# Optimizing a Trainium2 kernel written in Bass

```python
import math
import jax, jax.numpy as jnp
from jax import lax
import numpy as np

D_MODEL = 1024
BATCH = 1
SEQ = 512
DEPTH = 1

N_SUBLAYERS = 3
N_MOD = 3
D_FF = 2816
POOL_WINDOWS = (2, 4, 8, 16)
POOL_GROUPS = len(POOL_WINDOWS)
POOL_WIDTH = D_MODEL // 2
POOL_GROUP_DIM = POOL_WIDTH // POOL_GROUPS
N_HEADS = 8
QK_NOPE_DIM = 64
QK_ROPE_DIM = 32
V_HEAD_DIM = 64
QK_HEAD_DIM = QK_NOPE_DIM + QK_ROPE_DIM
Q_LORA_RANK = 384
KV_LORA_RANK = 256
MLA_WIDTH = N_HEADS * V_HEAD_DIM
ROPE_THETA = 10000.0
Q_BLOCK = 128
ATTN_SCALE = 1.0 / math.sqrt(QK_HEAD_DIM)
NORM_EPS = 1e-6
IN_SPLITS = (POOL_WIDTH, Q_LORA_RANK, KV_LORA_RANK, QK_ROPE_DIM, D_MODEL, D_MODEL)
IN_WIDTH = sum(IN_SPLITS)

kernel_name = "hybrid_pool_mla_macaron_adaln"

def rms_norm(x, g):
    xf = x.astype(jnp.float32)
    y = xf * lax.rsqrt(jnp.mean(xf * xf, axis=-1, keepdims=True) + NORM_EPS)
    return (y * g.astype(jnp.float32)).astype(x.dtype)

def modulate(h, shift, scale):
    return h * (1.0 + scale[:, None, :]) + shift[:, None, :]

def swiglu(h, w_in, w_out):
    gu = h @ w_in
    g, u = jnp.split(gu, 2, axis=-1)
    return (jax.nn.silu(g) * u) @ w_out

def rope_tables(positions):
    inv_freq = ROPE_THETA ** (-jnp.arange(0, QK_ROPE_DIM, 2, dtype=jnp.float32) / QK_ROPE_DIM)
    ang = positions.astype(jnp.float32)[..., None] * inv_freq
    ang = jnp.concatenate([ang, ang], axis=-1)
    return jnp.cos(ang), jnp.sin(ang)

def apply_rope(x, cos, sin):
    xf = x.astype(jnp.float32)
    x1, x2 = jnp.split(xf, 2, axis=-1)
    rot = jnp.concatenate([-x2, x1], axis=-1)
    return (xf * cos + rot * sin).astype(x.dtype)

def causal_multiscale_pool(u):
    B, S, _ = u.shape
    uf = u.astype(jnp.float32).reshape(B, S, POOL_GROUPS, POOL_GROUP_DIM)
    cs = jnp.pad(jnp.cumsum(uf, axis=1), ((0, 0), (1, 0), (0, 0), (0, 0)))
    t = jnp.arange(S)
    outs = []
    for g, w in enumerate(POOL_WINDOWS):
        hi = cs[:, 1:, g]
        lo = cs[:, jnp.maximum(t + 1 - w, 0), g]
        cnt = jnp.minimum(t + 1, w).astype(jnp.float32)
        outs.append((hi - lo) / cnt[None, :, None])
    pooled = jnp.stack(outs, axis=2)
    return (pooled - uf).astype(u.dtype)

def causal_mla_attention(q_nope, q_rope, k_nope, k_rope, v):
    S = q_nope.shape[1]
    outs = []
    for i in range(S // Q_BLOCK):
        q0, q1 = i * Q_BLOCK, (i + 1) * Q_BLOCK
        s = (jnp.einsum('bqhd,bkhd->bhqk', q_nope[:, q0:q1], k_nope[:, :q1])
             + jnp.einsum('bqhr,bkr->bhqk', q_rope[:, q0:q1], k_rope[:, :q1]))
        s = s.astype(jnp.float32) * ATTN_SCALE
        mask = jnp.arange(q1)[None, :] <= (q0 + jnp.arange(Q_BLOCK))[:, None]
        s = jnp.where(mask, s, jnp.float32(-1e30))
        p = jax.nn.softmax(s, axis=-1).astype(v.dtype)
        outs.append(jnp.einsum('bhqk,bkhd->bqhd', p, v[:, :q1]))
    return jnp.concatenate(outs, axis=1)

def setup_inputs(seed: int = 0) -> dict:
    key = jax.random.key(seed)
    ks = jax.random.split(key, 32)
    f32 = jnp.float32

    def w(k, shape, fan_in, gain=1.0):
        return jax.random.normal(k, shape, f32) * (gain * fan_in ** -0.5)

    def gain(k, shape):
        return jnp.ones(shape, f32) + 0.05 * jax.random.normal(k, shape, f32)

    L = DEPTH
    x = jax.random.normal(ks[0], (BATCH, SEQ, D_MODEL), f32)
    c = jax.random.normal(ks[1], (BATCH, D_MODEL), f32)
    offs = jax.random.randint(ks[2], (BATCH, 1), 0, 256, dtype=jnp.int32)
    positions = jnp.arange(SEQ, dtype=jnp.int32)[None, :] + offs
    return {
        "x": x,
        "c": c,
        "positions": positions,
        "w_ada": w(ks[3], (L, D_MODEL, N_SUBLAYERS * N_MOD * D_MODEL), D_MODEL, 0.5),
        "b_ada": 0.05 * jax.random.normal(ks[4], (L, N_SUBLAYERS * N_MOD * D_MODEL), f32),
        "norm_ffn1": gain(ks[5], (L, D_MODEL)),
        "w_ffn1_in": w(ks[6], (L, D_MODEL, 2 * D_FF), D_MODEL),
        "w_ffn1_out": w(ks[7], (L, D_FF, D_MODEL), D_FF),
        "norm_mix": gain(ks[8], (L, D_MODEL)),
        "w_in": w(ks[9], (L, D_MODEL, IN_WIDTH), D_MODEL),
        "pool_grp": w(ks[10], (L, POOL_GROUPS, POOL_GROUP_DIM, POOL_GROUP_DIM), POOL_GROUP_DIM),
        "pool_scale": gain(ks[11], (L, POOL_WIDTH)),
        "w_pool_proj": w(ks[12], (L, POOL_WIDTH, D_MODEL), POOL_WIDTH),
        "q_a_norm": gain(ks[13], (L, Q_LORA_RANK)),
        "w_q_up": w(ks[14], (L, Q_LORA_RANK, N_HEADS * QK_HEAD_DIM), Q_LORA_RANK),
        "kv_a_norm": gain(ks[15], (L, KV_LORA_RANK)),
        "w_kv_up": w(ks[16], (L, KV_LORA_RANK, N_HEADS * (QK_NOPE_DIM + V_HEAD_DIM)), KV_LORA_RANK),
        "q_norm_nope": gain(ks[17], (L, QK_NOPE_DIM)),
        "q_norm_rope": gain(ks[18], (L, QK_ROPE_DIM)),
        "k_norm_nope": gain(ks[19], (L, QK_NOPE_DIM)),
        "k_norm_rope": gain(ks[20], (L, QK_ROPE_DIM)),
        "w_mla_proj": w(ks[21], (L, MLA_WIDTH, D_MODEL), MLA_WIDTH),
        "w_out": w(ks[22], (L, D_MODEL, D_MODEL), D_MODEL),
        "norm_ffn2": gain(ks[23], (L, D_MODEL)),
        "w_ffn2_in": w(ks[24], (L, D_MODEL, 2 * D_FF), D_MODEL),
        "w_ffn2_out": w(ks[25], (L, D_FF, D_MODEL), D_FF),
    }

def reference(x, c, positions, w_ada, b_ada, norm_ffn1, w_ffn1_in, w_ffn1_out,
              norm_mix, w_in, pool_grp, pool_scale, w_pool_proj, q_a_norm, w_q_up,
              kv_a_norm, w_kv_up, q_norm_nope, q_norm_rope, k_norm_nope, k_norm_rope,
              w_mla_proj, w_out, norm_ffn2, w_ffn2_in, w_ffn2_out):
    B, S, D = x.shape
    cos, sin = rope_tables(positions)
    c_act = jax.nn.silu(c)
    split_pts = list(np.cumsum(IN_SPLITS)[:-1])

    for l in range(DEPTH):
        mod = (c_act @ w_ada[l] + b_ada[l]).reshape(B, N_SUBLAYERS, N_MOD, D)

        h = modulate(rms_norm(x, norm_ffn1[l]), mod[:, 0, 0], mod[:, 0, 1])
        x = x + 0.5 * mod[:, 0, 2][:, None, :] * swiglu(h, w_ffn1_in[l], w_ffn1_out[l])

        h = modulate(rms_norm(x, norm_mix[l]), mod[:, 1, 0], mod[:, 1, 1])
        u_pool, q_lat, kv_lat, k_rope, g_pool, g_mla = jnp.split(h @ w_in[l], split_pts, axis=-1)

        pooled = causal_multiscale_pool(u_pool).reshape(B, S, POOL_GROUPS, POOL_GROUP_DIM)
        pooled = jnp.einsum('bsgc,gcd->bsgd', pooled, pool_grp[l]).reshape(B, S, POOL_WIDTH)
        br_pool = (pooled * pool_scale[l]) @ w_pool_proj[l]

        q = (rms_norm(q_lat, q_a_norm[l]) @ w_q_up[l]).reshape(B, S, N_HEADS, QK_HEAD_DIM)
        q_nope, q_rope = q[..., :QK_NOPE_DIM], q[..., QK_NOPE_DIM:]
        kv = (rms_norm(kv_lat, kv_a_norm[l]) @ w_kv_up[l]).reshape(
            B, S, N_HEADS, QK_NOPE_DIM + V_HEAD_DIM)
        k_nope, v = kv[..., :QK_NOPE_DIM], kv[..., QK_NOPE_DIM:]
        q_nope = rms_norm(q_nope, q_norm_nope[l])
        k_nope = rms_norm(k_nope, k_norm_nope[l])
        q_rope = apply_rope(rms_norm(q_rope, q_norm_rope[l]), cos[:, :, None, :], sin[:, :, None, :])
        k_rope = apply_rope(rms_norm(k_rope, k_norm_rope[l]), cos, sin)
        attn = causal_mla_attention(q_nope, q_rope, k_nope, k_rope, v).reshape(B, S, MLA_WIDTH)
        br_mla = attn @ w_mla_proj[l]

        merged = jax.nn.sigmoid(g_pool) * br_pool + jax.nn.sigmoid(g_mla) * br_mla
        x = x + mod[:, 1, 2][:, None, :] * (merged @ w_out[l])

        h = modulate(rms_norm(x, norm_ffn2[l]), mod[:, 2, 0], mod[:, 2, 1])
        x = x + 0.5 * mod[:, 2, 2][:, None, :] * swiglu(h, w_ffn2_in[l], w_ffn2_out[l])

    return x


_drawn_inputs = setup_inputs


def setup_inputs(seed=0):
    import zlib

    import numpy as np

    out = dict(_drawn_inputs(seed))
    spreads = {}
    factors = {'norm_ffn1': 6.693,
     'norm_mix': 7.062,
     'pool_scale': 7.093,
     'q_a_norm': 8.0,
     'w_q_up': 2.83,
     'kv_a_norm': 8.0,
     'q_norm_nope': 8.0,
     'q_norm_rope': 8.0,
     'k_norm_nope': 8.0,
     'k_norm_rope': 8.0,
     'norm_ffn2': 7.54}
    for name, (base, spread) in spreads.items():
        noise = np.random.default_rng([zlib.crc32(name.encode()), seed]).standard_normal(out[name].shape)
        drawn = base * np.exp(spread * noise) if base else spread * noise
        out[name] = __import__('jax').numpy.asarray(drawn.astype(out[name].dtype))
    for name, factor in factors.items():
        out[name] = (out[name] * factor).astype(out[name].dtype)
    return out
```

```python
from contextlib import ExitStack

import concourse.bass as bass
from concourse import mybir

ALU = mybir.AluOpType
ACT = mybir.ActivationFunctionType
F32 = mybir.dt.float32
F32R = mybir.dt.float32r
AX_X = mybir.AxisListType.X

P = 128
D = 1024
S = 512
D_FF = 2816
EPS = 1e-6
KD = D // P
NF = D_FF // P
NFH = NF // 2
IN_ELEMS = 2 * KD * P
OUT_ELEMS = NFH * P
ADA_COLS = 512
ADA_GROUPS = 9 * D // ADA_COLS
ADA_START = 2 * D // ADA_COLS
FFN_CHUNKS = NF + 2 * KD
FIRST_CHUNK = [0, FFN_CHUNKS + 24]
FFN_USED = [0, FFN_CHUNKS + 4]
SLOT = 2048

HEADS = 8
NOPE = 64
ROPE = 32
HEAD = NOPE + ROPE
V_DIM = 64
Q_RANK = 384
KV_RANK = 256
LAT = Q_RANK + KV_RANK + ROPE
Q_TILES = Q_RANK // P
KV_TILES = KV_RANK // P
POOL_TILES = 4
TOK = S // P
ATTN_SCALE = 1.0 / HEAD ** 0.5
LAT_COLS = [(0, 256), (256, 256), (512, 160)]
MIX_CHUNK = FFN_CHUNKS
MIX_SIZES = [KD * n for _, n in LAT_COLS] + [SLOT, SLOT, KV_TILES * 1024, Q_TILES * 384, Q_TILES * 384 + 4 * P,
                                             SLOT, SLOT] + [SLOT] * 8 + [SLOT] * 2 + [SLOT] * 4
LAT_AT, UPOOL_AT, KV_AT, Q_AT, PP_AT, GATE_AT, MLA_AT, WOUT_AT = 0, 3, 5, 6, 8, 10, 18, 20
MASK_AT, QG_AT, KG_AT = 0, P, P + HEAD
CORR_AT = KG_AT + HEAD
FREQ_AT = CORR_AT + 16 * POOL_TILES
LG_AT = FREQ_AT + ROPE // 2
PS_AT = LG_AT + Q_TILES + KV_TILES
MIXC = PS_AT + POOL_TILES
TWO_PI = (6.28125, 0.0019350051879882812, 3.0199159819567e-07)
MAGIC = 1.5 * 2.0 ** 23


def program(nc, x_t, c_t, gains, b_ada, w_ada, w_ffn_in, w_ffn_out, w_mix, mix_consts, positions, consts, out):
    ctx = ExitStack()
    with ctx:
        cursor = [16512]

        def place(name, shape, dt=F32, at=None):
            size = 4
            for n in shape[1:]:
                size *= n
            if at is None:
                at = cursor[0]
                cursor[0] += (size + 31) // 32 * 32
            assert at + size <= 229344, (name, at + size)
            return nc.alloc_sbuf_tensor_at(name, shape, dt, offset=at)

        def sem(name):
            return ctx.enter_context(nc.semaphore(name))

        x = place("x", [P, KD, S])
        h_hi = place("h_hi", [P, KD, S], F32R)
        h_lo = place("h_lo", [P, KD, S], F32R)
        w_raw = [place(f"w_raw{i}", [P, SLOT]) for i in range(2)]
        w_hi = [place(f"w_hi{i}", [P, SLOT], F32R) for i in range(2)]
        w_lo = [place(f"w_lo{i}", [P, SLOT], F32R) for i in range(2)]
        ident = place("ident", [P, P])
        ones = place("ones", [P, P])
        mod = place("mod", [P, 72])
        bias_ada = place("bias_ada", [P, 72])
        gain = place("gain", [P, 3 * KD])
        c_raw = place("c_raw", [P, KD])
        c_act = place("c_act", [P, KD])
        gain_mod = place("gain_mod", [P, KD])
        out_gate = place("out_gate", [P, KD])
        var = place("var", [P, 4])
        std = place("std", [P, 4])
        rstd = place("rstd", [P, 4])
        newton = place("newton", [P, 4])
        warm = place("warm", [P, 8])
        scaled_at = cursor[0]
        scaled = place("scaled", [P, 2, S])
        h32 = place("h32", [P, 2, S])
        ssq = place("ssq", [P, S])
        ada_acc = place("ada_acc", [P, ADA_COLS])
        phase_at = cursor[0]
        silu_g = scaled[:, 0, :]
        prod = scaled[:, 1, :]
        square = scaled[:, 0, :]
        diag = h32[:, 0, :]

        ada_raw = place("ada_raw", [P, KD // 2, ADA_COLS], at=phase_at)
        act_at = phase_at + 4 * 4 * ADA_COLS
        ada_first = place("ada_first", [P, ADA_START, KD, ADA_COLS], at=act_at)
        act_hi = [place(f"act_hi{f}", [P, NF, S], F32R, at=act_at) for f in range(2)]
        act_lo = [place(f"act_lo{f}", [P, NF, S], F32R, at=act_at + 4 * NF * S) for f in range(2)]

        kib = 1024
        v_tok = place("v_tok", [P, TOK, HEADS * V_DIM], at=phase_at)
        br_pool = place("br_pool", [P, KD, S], at=phase_at + 8 * kib)
        u_pad = place("u_pad", [P, POOL_TILES, 16 + S], at=phase_at + 8 * kib)
        window = [place(f"window{i}", [P, 16 + S], at=phase_at + 8 * kib + 4 * (POOL_TILES + i) * (16 + S))
                  for i in range(2)]
        lat = place("lat", [P, TOK, LAT], at=phase_at + 24 * kib)
        lat_hi = place("lat_hi", [P, Q_TILES + KV_TILES, S], F32R, at=phase_at + 24 * kib + 4 * TOK * LAT)
        lat_lo = place("lat_lo", [P, Q_TILES + KV_TILES, S], F32R, at=phase_at + 34 * kib + 4 * TOK * LAT)
        group_hi = place("group_hi", [P, POOL_TILES, S], F32R, at=phase_at + 24 * kib)
        group_lo = place("group_lo", [P, POOL_TILES, S], F32R, at=phase_at + 32 * kib)
        q_t = place("q_t", [P, HEADS, S], at=phase_at + 24 * kib)
        k_t = place("k_t", [P, HEADS, S], at=phase_at + 40 * kib)
        attn_hi = place("attn_hi", [P, 4, S], F32R, at=phase_at + 24 * kib)
        attn_lo = place("attn_lo", [P, 4, S], F32R, at=phase_at + 32 * kib)
        qk_tok = place("qk_tok", [P, 2, TOK, HEADS, HEAD], at=phase_at + 56 * kib)
        attn_tok = place("attn_tok", [P, TOK, HEADS * V_DIM], at=phase_at + 56 * kib)
        p_tok = place("p_tok", [P, 10, P], at=phase_at + 64 * kib)
        p_t = place("p_t", [P, 10, P], at=phase_at + 69 * kib)
        q_now = place("q_now", [P, S], at=phase_at + 74 * kib)
        pooled_hi = place("pooled_hi", [P, POOL_TILES, S], F32R, at=phase_at + 80 * kib)
        pooled_lo = place("pooled_lo", [P, POOL_TILES, S], F32R, at=phase_at + 88 * kib)
        tanh_mla = place("tanh_mla", [P, KD, S], at=phase_at + 80 * kib)
        mixc = place("mixc", [P, MIXC], at=cursor[0] - 4096)
        cursor[0] = (cursor[0] - 4096 + 4 * MIXC + 31) // 32 * 32
        small_end = cursor[0]
        pos_int = place("pos_int", [P, TOK], mybir.dt.int32)
        cos = place("cos", [P, TOK, ROPE])
        sin = place("sin", [P, TOK, ROPE])
        mvar = place("mvar", [P, 3 * TOK * HEADS])
        mstd = place("mstd", [P, 3 * TOK * HEADS])
        mrstd = place("mrstd", [P, 3 * TOK * HEADS])
        mnewton = place("mnewton", [P, 3 * TOK * HEADS], at=scaled_at + 7168)
        assert cursor[0] <= phase_at, cursor[0] - phase_at
        spare = [96 * kib + phase_at]

        def place_small(name, shape, dt=F32):
            t = place(name, shape, dt, at=spare[0])
            spare[0] += 32
            return t

        row_max = place_small("row_max", [P, TOK])
        row_sum = place_small("row_sum", [P, TOK])
        row_inv = place_small("row_inv", [P, TOK])
        squares = place("squares", [P, 2, HEADS * HEAD], at=scaled_at)
        rot_a = place("rot_a", [P, TOK, HEADS, ROPE], at=scaled_at)
        rot_b = place("rot_b", [P, TOK, HEADS, ROPE], at=scaled_at + 4096)
        krot = place("krot", [P, 2, TOK, ROPE], at=scaled_at + 6144)
        angle = [place(f"angle{i}", [P, TOK, ROPE // 2], at=scaled_at + 6144 + 256 * i) for i in range(4)]

        bank = [ctx.enter_context(nc.psum_tensor(f"bank{i}", [P, S], F32)) for i in range(8)]
        ADA_BANK, STAT_BANK = bank[6], bank[7]

        const_in = sem("const_in")
        x_in = sem("x_in")
        raw_in = [sem(f"raw_in{i}") for i in range(2)]
        ada_first_in = [sem(f"ada_first_in{i}") for i in range(ADA_START)]
        ada_in = [sem(f"ada_in{i}") for i in range(4)]
        hi_done = sem("hi_done")
        lo_done = sem("lo_done")
        pe_used = sem("pe_used")
        c_ready = sem("c_ready")
        ones_ready = sem("ones_ready")
        ada_step = sem("ada_step")
        ada_summed = sem("ada_summed")
        mod_ready = sem("mod_ready")
        sq_done = sem("sq_done")
        sq_added = sem("sq_added")
        stat_ready = sem("stat_ready")
        var_ready = sem("var_ready")
        std_ready = sem("std_ready")
        small = sem("small")
        diag_ready = sem("diag_ready")
        rstd_wide = sem("rstd_wide")
        scaled_ready = sem("scaled_ready")
        h32_ready = sem("h32_ready")
        h_hi_ready = sem("h_hi_ready")
        h_ready = [sem("h_ready_even"), sem("h_ready_odd")]
        gu_ready = sem("gu_ready")
        silu_done = sem("silu_done")
        gu_evac = sem("gu_evac")
        act_hi_done = sem("act_hi_done")
        act_done = sem("act_done")
        out_ready = sem("out_ready")
        out_evac = sem("out_evac")
        stored = sem("stored")

        mixc_in = sem("mixc_in")
        mixc_scaled = sem("mixc_scaled")
        lat_ready = sem("lat_ready")
        lat_evac = sem("lat_evac")
        u_ready = sem("u_ready")
        u_evac = sem("u_evac")
        msq_done = sem("msq_done")
        msq_used = sem("msq_used")
        mvar_ready = sem("mvar_ready")
        mstd_ready = sem("mstd_ready")
        latn_ready = sem("latn_ready")
        lat_t_ready = sem("lat_t_ready")
        lat_hi_done = sem("lat_hi_done")
        lat_lo_done = sem("lat_lo_done")
        angle_ready = sem("angle_ready")
        trig_ready = sem("trig_ready")
        kv_ready = sem("kv_ready")
        kv_evac = sem("kv_evac")
        q_ready = sem("q_ready")
        q_evac = sem("q_evac")
        pooled_ready = sem("pooled_ready")
        pooled_hi_done = sem("pooled_hi_done")
        pooled_lo_done = sem("pooled_lo_done")
        group_ready = sem("group_ready")
        group_hi_done = sem("group_hi_done")
        group_lo_done = sem("group_lo_done")
        proj_ready = sem("proj_ready")
        proj_evac = sem("proj_evac")
        qk_tok_ready = sem("qk_tok_ready")
        qk_t_ready = sem("qk_t_ready")
        q_t_evac = sem("q_t_evac")
        k_t_evac = sem("k_t_evac")
        q_now_ready = sem("q_now_ready")
        scores_ready = sem("scores_ready")
        max_ready = sem("max_ready")
        p_ready = sem("p_ready")
        p_t_ready = sem("p_t_ready")
        p_t_act = sem("p_t_act")
        p_t_dve = sem("p_t_dve")
        gate_ready = sem("gate_ready")
        tanh_done = sem("tanh_done")
        pv_ready = sem("pv_ready")
        pv_evac = sem("pv_evac")
        attn_t_ready = sem("attn_t_ready")
        attn_hi_done = sem("attn_hi_done")
        attn_lo_done = sem("attn_lo_done")
        mla_ready = sem("mla_ready")
        merged_ready = sem("merged_ready")
        merged_hi_done = sem("merged_hi_done")
        merged_lo_done = sem("merged_lo_done")
        gated = sem("gated")
        mla_gated = sem("mla_gated")
        inv_done = sem("inv_done")
        k_rope_done = sem("k_rope_done")

        block = ctx.enter_context(nc.Block())

        chunk_used = ([(lat_ready, TOK * (c + 1)) for c in range(3)] + [(u_ready, 2 * c + 2) for c in range(2)]
                      + [(kv_ready, 8), (q_ready, 4), (group_ready, 4)] + [(proj_ready, 4 * c + 4) for c in range(2)]
                      + [(gate_ready, 2 * c + 2) for c in range(HEADS)] + [(mla_ready, 4 * c + 4) for c in range(2)]
                      + [(pe_used, FFN_CHUNKS + c + 1) for c in range(4)])

        @block.sync
        def _(sp):
            def load_w(src, slot, size, lo_count):
                if lo_count is not None:
                    sp.wait_ge(lo_done, lo_count)
                sp.dma_start(w_raw[slot][:, 0:size], src).then_inc(raw_in[slot], 16)

            def load_ada(group, kt, wait=True):
                if wait:
                    sp.wait_ge(ada_step, 8 * (group - ADA_START) + kt - 3)
                sp.dma_start(ada_raw[:, kt % 4, :], w_ada[group, kt]).then_inc(ada_in[kt % 4], 16)

            def half_ada(group, s):
                for kt in range(4):
                    load_ada(group + s, 4 - 4 * s + kt)

            def ffn(f, after):
                n0 = FIRST_CHUNK[f]

                def up(i, last):
                    for s in range(2):
                        j = 2 * i + s
                        if last:
                            load_w(w_ffn_out[f, s], s, OUT_ELEMS, n0 + j + 1)
                        else:
                            load_w(w_ffn_in[f, j + 2], s, IN_ELEMS, n0 + j + 1)
                        if f == 0:
                            half_ada(ADA_START + i, s)

                with sp.Fori(0, NFH - 1) as i:
                    up(i, False)
                up(NFH - 1, True)

                def down(i, ada, last):
                    for s in range(4):
                        q = 4 * i + s
                        if last and s >= 2:
                            if after:
                                after(s - 2)
                        else:
                            load_w(w_ffn_out[f, q + 2], s % 2, OUT_ELEMS, n0 + NF + q + 1)
                        if ada and s in ada:
                            half_ada(ADA_START + NFH + i, s // 2)

                with sp.Fori(0, 2) as i:
                    down(i, (0, 2) if f == 0 else None, False)
                down(2, (0,) if f == 0 else None, False)
                down(3, None, True)

            sp.dma_start(x[:, :, :], x_t).then_inc(x_in, 16)
            sp.dma_start(c_raw[:, :], c_t).then_inc(const_in, 16)
            sp.dma_start(gain[:, :], gains).then_inc(const_in, 16)
            sp.dma_start(bias_ada[:, :], b_ada).then_inc(const_in, 16)
            sp.dma_start(ident[:, :], consts[:, 0:P]).then_inc(const_in, 16)
            for g in range(ADA_START):
                for half in range(2):
                    kts = slice(4 * half, 4 * half + 4)
                    sp.dma_start(ada_first[:, g, kts, :], w_ada[g, kts].rearrange("k p c -> p k c"))\
                        .then_inc(ada_first_in[g], 16)
                if g >= ADA_START - 2:
                    load_w(w_ffn_in[0, g % 2], g % 2, IN_ELEMS, None)
            for kt in range(4):
                load_ada(ADA_START, kt, False)
            def mix_w(k):
                load_w(w_mix[k, :, 0:MIX_SIZES[k]], k % 2, MIX_SIZES[k], MIX_CHUNK + k - 1)

            ffn(0, mix_w)
            sp.wait_ge(stat_ready, 2)
            sp.dma_start(mixc[:, :], mix_consts).then_inc(mixc_in, 16)
            sp.dma_start(pos_int[:, :], positions).then_inc(mixc_in, 16)
            for k in range(2, GATE_AT):
                mix_w(k)
            with sp.Fori(GATE_AT // 2, len(MIX_SIZES) // 2) as i:
                for s in range(2):
                    load_w(w_mix[2 * i + s], s, SLOT, MIX_CHUNK + 2 * i + s - 1)
            for s in range(2):
                load_w(w_ffn_in[1, s], s, IN_ELEMS, FIRST_CHUNK[1] + s - 1)
            ffn(1, None)
            with sp.Fori(0, KD) as m:
                sp.wait_ge(out_evac, 2 * KD + m + 3)
                sp.dma_start(out[m], x[:, bass.ds(m, 1), :].rearrange("p a s -> p (a s)")).then_inc(stored, 16)
            sp.wait_ge(stored, 16 * KD)

        @block.tensor
        def _(pe):
            def product(dst, stationary, moving, start, stop):
                (a_hi, a_lo), (b_hi, b_lo) = stationary, moving
                nc.tensor.matmul(dst, a_hi, b_hi, start=start, stop=False)
                nc.tensor.matmul(dst, a_lo, b_hi, start=False, stop=False)
                return nc.tensor.matmul(dst, a_hi, b_lo, start=False, stop=stop)

            def w_tile(slot, t):
                cols = slice(t * P, (t + 1) * P)
                return w_hi[slot][:, cols], w_lo[slot][:, cols]

            def reduce_ada(group, acc_steps):
                pe.wait_ge(ada_step, acc_steps)
                pe.wait_ge(mod_ready, group)
                for c in range(4):
                    last = nc.tensor.matmul(ADA_BANK[:, bass.ds(4 * group + c, 1)], ada_acc[:, c * P:(c + 1) * P],
                                            ones[:, 0:1], start=True, stop=True)
                last.then_inc(ada_summed, 1)

            def first_ada(group):
                pe.wait_ge(ada_first_in[group], 32)
                if group:
                    pe.wait_ge(mod_ready, group)
                for c in range(4):
                    for kt in range(KD):
                        last = nc.tensor.matmul(ADA_BANK[:, 4 * group + c:4 * group + c + 1],
                                                ada_first[:, group, kt, c * P:(c + 1) * P], c_act[:, kt:kt + 1],
                                                start=kt == 0, stop=kt == KD - 1)
                last.then_inc(ada_summed, 1)

            def norm(l):
                pe.wait_ge(sq_added, (KD - 1) * (l + 1))
                pe.wait_ge(sq_done, KD * (l + 1))
                for t in range(4):
                    cols = slice(t * P, (t + 1) * P)
                    nc.tensor.matmul(STAT_BANK[:, t:t + 1], ssq[:, cols], ones[:, 0:1], start=True, stop=False)
                    last = nc.tensor.matmul(STAT_BANK[:, t:t + 1], square[:, cols], ones[:, 0:1],
                                            start=False, stop=True)
                last.then_inc(stat_ready, 1)
                pe.wait_ge(diag_ready, l + 1)
                nc.tensor.matmul(bank[4][:, :], ones[:, :], diag, start=True, stop=True).then_inc(rstd_wide, 1)

            def ffn(f):
                n0 = FIRST_CHUNK[f]

                def up(i, first):
                    for s in range(2):
                        j = 2 * i + s
                        pe.wait_ge(lo_done, n0 + j + 1)
                        pe.wait_ge(gu_evac, NF * f + j + 1)
                        for k in range(KD):
                            if first and s == 0:
                                pe.wait_ge(h_ready[k % 2], KD * f + k // 2 + 1)
                            if f == 0 and not first and s == 0 and k == KD // 2:
                                reduce_ada(ADA_START + i - 1, 8 * i)
                            for gu in range(2):
                                last = product(bank[2 * s + gu][:, :], w_tile(s, gu * KD + k),
                                               (h_hi[:, k, :], h_lo[:, k, :]), k == 0, k == KD - 1)
                        last.then_inc(pe_used, 1)

                up(0, True)
                with pe.Fori(1, NFH) as i:
                    up(i, False)

                def down(i):
                    for mm in range(2):
                        m = 2 * i + mm
                        pe.wait_ge(out_evac, KD * 2 * f + m + 1)
                        for half in range(2):
                            pe.wait_ge(lo_done, n0 + NF + 2 * m + half + 1)
                            pe.wait_ge(act_done, NF * f + NFH * (half + 1))
                            for k in range(NFH):
                                last = product(bank[4 + mm][:, :], w_tile(half, k),
                                               (act_hi[f][:, half * NFH + k, :], act_lo[f][:, half * NFH + k, :]),
                                               half + k == 0, half * k == NFH - 1)
                            last.then_inc(pe_used, 1)
                            if f == 0 and mm == 0 and half == 0:
                                reduce_ada(ADA_START + NFH + i - 1, 8 * (NFH + i))

                with pe.Fori(0, 4) as i:
                    down(i)

            def h_pair(k, cols=slice(0, S)):
                return h_hi[:, k, cols], h_lo[:, k, cols]

            def toks(t):
                return slice(t * P, (t + 1) * P)

            def chunk(k):
                pe.wait_ge(lo_done, MIX_CHUNK + k + 1)
                return (MIX_CHUNK + k) % 2

            def w_cols(slot, a, n):
                return w_hi[slot][:, a:a + n], w_lo[slot][:, a:a + n]

            def mixer():
                for cg, (_, n) in enumerate(LAT_COLS):
                    slot = chunk(LAT_AT + cg)
                    order = ([(t, k) for k in range(KD) for t in range(TOK)] if cg == 0
                             else [(t, k) for t in range(TOK) for k in range(KD)])
                    for t, k in order:
                        if cg == 0 and t == 0:
                            pe.wait_ge(h_ready[k % 2], KD // 2 + k // 2 + 1)
                        if cg == 2 and k == 0:
                            pe.wait_ge(lat_evac, t + 1)
                        last = product(bank[(4 * cg + t) % 8][:, 0:n], h_pair(k, toks(t)),
                                       w_cols(slot, k * n, n), k == 0, k == KD - 1)
                        if k == KD - 1:
                            last.then_inc(lat_ready, 1)
                for c in range(2):
                    slot = chunk(UPOOL_AT + c)
                    for g in range(2):
                        pe.wait_ge(lat_evac, TOK + 2 * c + g + 1)
                        for k in range(KD):
                            last = product(bank[4 + 2 * c + g][:, :], w_tile(slot, g * KD + k), h_pair(k),
                                           k == 0, k == KD - 1)
                        last.then_inc(u_ready, 1)
                pe.wait_ge(latn_ready, 1)
                pe.wait_ge(lat_evac, 3 * TOK)
                pe.wait_ge(u_evac, 1)
                for r in range(Q_TILES + KV_TILES):
                    ft = (r + Q_TILES) % (Q_TILES + KV_TILES)
                    for t in range(TOK):
                        last = nc.tensor.transpose(bank[r][:, toks(t)], lat[:, t, ft * P:(ft + 1) * P], ident[:, :])
                    last.then_inc(lat_t_ready, 1)
                slot = chunk(KV_AT)
                pe.wait_ge(u_evac, 4)
                pe.wait_ge(lat_lo_done, Q_TILES + KV_TILES)
                for kv in range(2):
                    for t in range(TOK):
                        for k in range(KV_TILES):
                            last = product(bank[(5 + 4 * kv + t) % 8][:, :],
                                           (lat_hi[:, Q_TILES + k, toks(t)], lat_lo[:, Q_TILES + k, toks(t)]),
                                           w_cols(slot, k * 1024 + kv * 512, 512), k == 0, k == KV_TILES - 1)
                        last.then_inc(kv_ready, 1)
                for c in range(2):
                    slot = chunk(Q_AT + c)
                    for t in range(TOK):
                        pe.wait_ge(kv_evac, 4 * c + t + 1)
                        for k in range(Q_TILES):
                            last = product(bank[(5 + 4 * c + t) % 8][:, 0:384],
                                           (lat_hi[:, k, toks(t)], lat_lo[:, k, toks(t)]),
                                           w_cols(slot, k * 384, 384), k == 0, k == Q_TILES - 1)
                        last.then_inc(q_ready, 1)
                for g in range(POOL_TILES):
                    pe.wait_ge(q_evac, g + 1)
                    pe.wait_ge(pooled_lo_done, g + 1)
                    last = product(bank[(5 + g) % 8][:, :], w_cols(slot, Q_TILES * 384 + g * P, P),
                                   (pooled_hi[:, g, :], pooled_lo[:, g, :]), True, True)
                    last.then_inc(group_ready, 1)
                for m in range(KD):
                    if m % 4 == 0:
                        slot = chunk(PP_AT + m // 4)
                    if m < 4:
                        pe.wait_ge(q_evac, 4 + m + 1)
                    for k in range(POOL_TILES):
                        if m == 0:
                            pe.wait_ge(group_lo_done, k + 1)
                        last = product(bank[(1 + m) % 8][:, :], w_tile(slot, m % 4 * 4 + k),
                                       (group_hi[:, k, :], group_lo[:, k, :]), k == 0, k == POOL_TILES - 1)
                    last.then_inc(proj_ready, 1)
                for h in range(HEADS):
                    for qk in range(2):
                        r = 2 * h + qk
                        if r < 8:
                            pe.wait_ge(proj_evac, r + 1)
                        else:
                            pe.wait_ge((q_t_evac, k_t_evac)[qk], h - 3)
                        pe.wait_ge(qk_tok_ready, 2)
                        for t in range(TOK):
                            last = nc.tensor.transpose(bank[(1 + r) % 8][0:HEAD, toks(t)], qk_tok[:, qk, t, h, :],
                                                       ident[:, :])
                        last.then_inc(qk_t_ready, 1)
                pe.wait_ge(q_t_evac, HEADS)
                pe.wait_ge(k_t_evac, HEADS)

                def head(i, s):
                    h = 2 * i + s
                    pe.wait_ge(q_now_ready, h + 1)
                    for qt in range(TOK):
                        nc.tensor.matmul(bank[qt][:, 0:(qt + 1) * P], q_now[0:HEAD, toks(qt)],
                                         k_t[0:HEAD, bass.ds(h, 1), 0:(qt + 1) * P], start=True, stop=False)
                        nc.tensor.matmul(bank[qt][:, toks(qt)], ident[:, :], mixc[:, MASK_AT:MASK_AT + P],
                                         start=False, stop=True).then_inc(scores_ready, 1)
                    pe.wait_ge(lo_done, MIX_CHUNK + GATE_AT + h + 1)

                    def gate(g):
                        for k in range(KD):
                            last = product(bank[4 + g][:, :], w_tile(s, g * KD + k), h_pair(k), k == 0, k == KD - 1)
                        return last

                    gate(0).then_inc(gate_ready, 1)
                    pe.wait_ge(p_ready, TOK * h + TOK)
                    for b in range(10):
                        last = nc.tensor.transpose(bank[b // 4][:, toks(b % 4)], p_tok[:, b, :], ident[:, :])
                        if b % 4 == 3 or b == 9:
                            last.then_inc(p_t_ready, 1)
                    last = gate(1)
                    last.then_inc(gate_ready, 1)
                    pe.wait_ge(p_t_act, h + 1)
                    pe.wait_ge(p_t_dve, 2 * h + 2)
                    for qt in range(TOK):
                        for kt in range(qt + 1):
                            last = nc.tensor.matmul(bank[6][:, qt * V_DIM:(qt + 1) * V_DIM],
                                                    p_t[:, qt * (qt + 1) // 2 + kt, :],
                                                    v_tok[:, kt, bass.ds(h * V_DIM, V_DIM)],
                                                    start=kt == 0, stop=kt == qt)
                    last.then_inc(pv_ready, 1)

                with pe.Fori(0, HEADS // 2) as i:
                    for s in range(2):
                        head(i, s)
                pe.wait_ge(pv_evac, HEADS)
                for f in range(4):
                    for t in range(TOK):
                        last = nc.tensor.transpose(bank[f][:, toks(t)], attn_tok[:, t, f * P:(f + 1) * P], ident[:, :])
                    last.then_inc(attn_t_ready, 1)
                for m in range(KD):
                    if m % 4 == 0:
                        slot = chunk(MLA_AT + m // 4)
                    if m < 2:
                        pe.wait_ge(tanh_done, 2 * HEADS - 1 + m)
                    for k in range(4):
                        if m == 0:
                            pe.wait_ge(attn_lo_done, k + 1)
                        last = product(bank[(4 + m) % 8][:, :], w_tile(slot, m % 4 * 4 + k),
                                       (attn_hi[:, k, :], attn_lo[:, k, :]), k == 0, k == 3)
                    last.then_inc(mla_ready, 1)
                pe.wait_ge(merged_ready, 2)
                for c in range(4):
                    slot = chunk(WOUT_AT + c)
                    for g in range(2):
                        m = 2 * c + g
                        if m >= 4:
                            pe.wait_ge(out_evac, KD + m - 1)
                        for k in range(KD):
                            if m == 0:
                                pe.wait_ge(merged_lo_done, k + 1)
                            last = product(bank[4 + m % 4][:, :], w_tile(slot, g * KD + k), h_pair(k),
                                           k == 0, k == KD - 1)
                    last.then_inc(pe_used, 1)

            pe.wait_ge(ones_ready, 1)
            norm(0)
            pe.wait_ge(c_ready, 1)
            for g in range(ADA_START):
                first_ada(g)
            ffn(0)
            norm(1)
            mixer()
            norm(2)
            ffn(1)

        @block.scalar
        def _(act):
            def split(pair, slot, size, used=None):
                act.wait_ge(raw_in[slot], 16 * (pair + 1))
                if used:
                    act.wait_ge(*used)
                nc.scalar.activation(w_hi[slot][:, 0:size], w_raw[slot][:, 0:size], ACT.Copy).then_inc(hi_done, 1)

            def load_table(n, func):
                nc.scalar.activation(warm[:, n:n + 1], ident[:, 0:1], func)

            def square_x(m, count):
                act.wait_ge(sq_added, count)
                nc.scalar.activation(square, x[:, bass.ds(m, 1), :], ACT.Square).then_inc(sq_done, 1)

            def norm(l):
                act.wait_ge(var_ready, l + 1)
                nc.scalar.activation(std[:, :], var[:, :], ACT.Sqrt).then_inc(std_ready, 1)
                load_table(2 + l, (ACT.Silu, ACT.Sqrt, ACT.Silu)[l])
                shift = 3 * KD * l
                for m in range(KD):
                    act.wait_ge(scaled_ready, KD * l + m + 1)
                    nc.scalar.activation(h_hi[:, m, :], scaled[:, m % 2, :], ACT.Identity,
                                         scale=gain_mod[:, m:m + 1], bias=mod[:, shift + m:shift + m + 1])\
                        .then_inc(h_hi_ready, 1)

            def mix_split(k):
                used = chunk_used[k - 2] if k >= 2 else (pe_used, FFN_CHUNKS - 1 + k)
                split((MIX_CHUNK + k) // 2, k % 2, MIX_SIZES[k], used)

            def mixer():
                def copy(dst, src, done):
                    nc.scalar.activation(dst, src, ACT.Copy).then_inc(done, 1)

                def lat_out(r):
                    at, n = LAT_COLS[r // TOK]
                    act.wait_ge(lat_ready, r + 1)
                    copy(lat[:, r % TOK, at:at + n], bank[r % 8][:, 0:n], lat_evac)

                def u_out(g):
                    act.wait_ge(u_ready, g + 1)
                    copy(u_pad[:, g, 16:16 + S], bank[4 + g][:, :], u_evac)

                for c in range(3):
                    mix_split(c + 1)
                    for t in range(TOK):
                        lat_out(TOK * c + t)
                act.wait_ge(h_ready[0], KD)
                act.wait_ge(h_ready[1], KD)
                act.wait_ge(lat_evac, 3 * TOK)
                for r in range(2):
                    act.wait_ge(msq_used, r)
                    nc.scalar.activation(squares[:, :, 0:LAT], lat[:, 2 * r:2 * r + 2, :], ACT.Square)\
                        .then_inc(msq_done, 1)
                act.wait_ge(mvar_ready, 1)
                nc.scalar.activation(mstd[:, 0:3 * TOK], mvar[:, 0:3 * TOK], ACT.Sqrt).then_inc(mstd_ready, 1)
                mix_split(4)
                u_out(0)
                u_out(1)
                act.wait_ge(angle_ready, 1)
                nc.scalar.activation(sin[:, :, 0:16], angle[0][:, :, :], ACT.Sin, scale=-1.0).then_inc(trig_ready, 1)
                nc.scalar.activation(sin[:, :, 16:32], angle[0][:, :, :], ACT.Sin).then_inc(trig_ready, 1)
                nc.scalar.activation(cos[:, :, 0:16], angle[1][:, :, :], ACT.Sin).then_inc(trig_ready, 1)
                nc.scalar.activation(cos[:, :, 16:32], angle[1][:, :, :], ACT.Sin).then_inc(trig_ready, 1)
                mix_split(5)
                u_out(2)
                u_out(3)
                for r in range(Q_TILES + KV_TILES):
                    ft = (r + Q_TILES) % (Q_TILES + KV_TILES)
                    act.wait_ge(lat_t_ready, r + 1)
                    nc.scalar.activation(lat_hi[:, ft, :], bank[r][:, :], ACT.Copy, scale=mixc[:, LG_AT + ft:LG_AT + ft + 1])\
                        .then_inc(lat_hi_done, 1)
                mix_split(6)
                for r in range(8):
                    kv, t = r // 4, r % 4
                    act.wait_ge(kv_ready, r + 1)
                    src = bank[(5 + r) % 8][:, :]
                    if kv == 0:
                        copy(qk_tok[:, 1, t, :, 0:NOPE], src.rearrange("p (h d) -> p h d", h=HEADS), kv_evac)
                    else:
                        copy(v_tok[:, t, :], src, kv_evac)
                mix_split(7)

                def head_squares(qk, half, width):
                    act.wait_ge(msq_used, 4 - 2 * qk + half)
                    buf = squares[:, :, 0:HEADS * width].rearrange("p t (h d) -> p t h d", h=HEADS)
                    for t in range(2):
                        ins = nc.scalar.activation(buf[:, t], qk_tok[:, qk, 2 * half + t, :, 0:width], ACT.Square)
                    ins.then_inc(msq_done, 1)

                act.wait_ge(kv_evac, 8)
                head_squares(1, 0, NOPE)
                head_squares(1, 1, NOPE)

                def q_out(r):
                    c, t = r // 4, r % 4
                    act.wait_ge(q_ready, r + 1)
                    copy(qk_tok[:, 0, t, 4 * c:4 * c + 4, :],
                         bank[(5 + r) % 8][:, 0:384].rearrange("p (h d) -> p h d", h=4), q_evac)

                for r in range(4):
                    q_out(r)
                for g in range(POOL_TILES):
                    act.wait_ge(pooled_ready, g + 1)
                    copy(pooled_hi[:, g, :], window[g % 2][:, 0:S], pooled_hi_done)
                for r in range(4, 8):
                    q_out(r)
                mix_split(8)
                for g in range(POOL_TILES):
                    act.wait_ge(group_ready, g + 1)
                    nc.scalar.activation(group_hi[:, g, :], bank[(5 + g) % 8][:, :], ACT.Copy,
                                         scale=mixc[:, PS_AT + g:PS_AT + g + 1]).then_inc(group_hi_done, 1)
                mix_split(9)
                act.wait_ge(q_evac, 8)
                head_squares(0, 0, HEAD)
                head_squares(0, 1, HEAD)
                act.wait_ge(mvar_ready, 2)
                nc.scalar.activation(mstd[:, :], mvar[:, :], ACT.Sqrt).then_inc(mstd_ready, 1)
                load_table(6, ACT.Exp)
                for m in range(KD):
                    if m == 4:
                        mix_split(10)
                    act.wait_ge(proj_ready, m + 1)
                    copy(br_pool[:, m, :], bank[(1 + m) % 8][:, :], proj_evac)
                for h in range(HEADS):
                    act.wait_ge(qk_t_ready, 2 * h + 1)
                    copy(q_t[0:HEAD, h, :], bank[(1 + 2 * h) % 8][0:HEAD, :], q_t_evac)
                act.wait_ge(q_t_evac, HEADS)

                def head(i, s, half):
                    h = HEADS // 2 * half + 2 * i + s
                    copy(q_now[0:HEAD, :], q_t[0:HEAD, bass.ds(h, 1), :].rearrange("p a s -> p (a s)"), q_now_ready)
                    for qt in range(TOK):
                        at = qt * (qt + 1) // 2
                        act.wait_ge(max_ready, TOK * h + qt + 1)
                        nc.scalar.activation(p_tok[:, at:at + qt + 1, :].rearrange("p b q -> p (b q)"),
                                             bank[qt][:, 0:(qt + 1) * P], ACT.Exp, bias=row_max[:, qt:qt + 1],
                                             accum_out=row_sum[:, qt:qt + 1]).then_inc(p_ready, 1)

                    def gate(g):
                        act.wait_ge(gate_ready, 2 * h + g + 1)
                        if half:
                            dst = tanh_mla[:, bass.ds(2 * (2 * i + s) + g, 1), :].rearrange("p a s -> p (a s)")
                        else:
                            dst = scaled[:, g, :]
                        nc.scalar.activation(dst, bank[4 + g][:, :], ACT.Tanh, scale=0.5).then_inc(tanh_done, 1)

                    gate(0)
                    split((MIX_CHUNK + GATE_AT) // 2 + HEADS // 4 * half + i + (s + 1) // 2, 1 - s, SLOT)
                    act.wait_ge(p_t_ready, 3 * h + 2)
                    copy(p_t[:, 4:8, :].rearrange("p b q -> p (b q)"), bank[1][:, :], p_t_act)
                    gate(1)

                for half in range(2):
                    with act.Fori(0, HEADS // 4) as i:
                        for s in range(2):
                            head(i, s, half)
                for f in range(4):
                    act.wait_ge(attn_t_ready, f + 1)
                    copy(attn_hi[:, f, :], bank[f][:, :], attn_hi_done)
                for m in range(KD):
                    if m % 4 == 0:
                        mix_split(19 + m // 4)
                    act.wait_ge(merged_ready, m + 1)
                    copy(h_hi[:, m, :], h32[:, m % 2, :], merged_hi_done)
                load_table(7, ACT.Sqrt)
                for c in range(4):
                    if c < 3:
                        mix_split(21 + c)
                    else:
                        split(FIRST_CHUNK[1] // 2, 0, IN_ELEMS, (pe_used, FFN_USED[1] - 1))
                    for g in range(2):
                        m = 2 * c + g
                        act.wait_ge(out_evac, KD + m + 3)
                        square_x(m, 2 * (KD - 1) + m)

            def ffn(f, after):
                n0, u0 = FIRST_CHUNK[f], FFN_USED[f]

                def up(i, first, last):
                    for s in range(2):
                        j = 2 * i + s
                        split((n0 + s + 1) // 2 + i, 1 - s, OUT_ELEMS if last and s else IN_ELEMS,
                              (pe_used, u0 + j) if not (first and f == 0 and s == 0) else None)
                        act.wait_ge(pe_used, u0 + j + 1)
                        act.wait_ge(gu_evac, NF * f + j + 2)
                        nc.scalar.activation(silu_g, bank[2 * s][:, :], ACT.Silu).then_inc(silu_done, 1)
                        act.wait_ge(gu_evac, NF * f + j + 3)
                        nc.scalar.activation(act_hi[f][:, bass.ds(j, 1), :], prod, ACT.Copy).then_inc(act_hi_done, 1)

                up(0, True, False)
                with act.Fori(1, NFH - 1) as i:
                    up(i, False, False)
                up(NFH - 1, False, True)

                if f == 0:
                    load_table(0, ACT.Sqrt)

                def down(i, last):
                    for s in range(4):
                        q = NF + 4 * i + s
                        if not (last and s == 3):
                            split((n0 + NF + s + 1) // 2 + 2 * i, (s + 1) % 2, OUT_ELEMS, (pe_used, u0 + q))
                        elif after:
                            after()
                        if s % 2:
                            m = 2 * i + s // 2
                            act.wait_ge(out_evac, KD * 2 * f + m + 3)
                            if f == 0:
                                square_x(m, KD - 1 + m)

                with act.Fori(0, 3) as i:
                    down(i, False)
                down(3, True)

            act.wait_ge(const_in, 64)
            nc.scalar.activation(c_act[:, :], c_raw[:, :], ACT.Silu).then_inc(c_ready, 1)
            act.wait_ge(x_in, 16)
            nc.scalar.activation(square, x[:, 0, :], ACT.Square).then_inc(sq_done, 1)
            with act.Fori(1, KD) as m:
                square_x(m, m)
            norm(0)
            split(0, 0, IN_ELEMS)
            ffn(0, lambda: mix_split(0))
            norm(1)
            mixer()
            norm(2)
            ffn(1, None)

        @block.vector
        def _(dve):
            links = [0]

            def link(ins):
                links[0] += 1
                ins.then_inc(small, 1)
                dve.wait_ge(small, links[0])

            def split(n, slot, size):
                dve.wait_ge(hi_done, n + 1)
                nc.vector.tensor_tensor(w_lo[slot][:, 0:size], w_raw[slot][:, 0:size],
                                        w_hi[slot][:, 0:size].bitcast(F32), ALU.subtract).then_inc(lo_done, 1)

            def add_ada(group, kts):
                for kt in kts:
                    dve.wait_ge(ada_in[kt % 4], 16 * (2 * (group - ADA_START) + kt // 4 + 1))
                    raw = ada_raw[:, kt % 4, :]
                    if kt == 0:
                        dve.wait_ge(ada_summed, group)
                        nc.vector.tensor_scalar(ada_acc[:, :], raw, c_act[:, 0:1], None, ALU.mult)\
                            .then_inc(ada_step, 1)
                    else:
                        dve.wait_ge(ada_step, 8 * (group - ADA_START) + kt)
                        nc.vector.scalar_tensor_tensor(out=ada_acc[:, :], in0=raw,
                                                       scalar=c_act[:, kt:kt + 1], in1=ada_acc[:, :],
                                                       op0=ALU.mult, op1=ALU.add).then_inc(ada_step, 1)

            def keep_mod(group):
                dve.wait_ge(ada_summed, group + 1)
                cols = bass.ds(4 * group, 4)
                nc.vector.tensor_tensor(mod[:, cols], ADA_BANK[:, cols], bias_ada[:, cols], ALU.add)\
                    .then_inc(mod_ready, 1)

            def norm(l):
                dve.wait_ge(stat_ready, l + 1)
                nc.vector.tensor_scalar(var[:, :], STAT_BANK[:, 0:4], 1.0 / D, EPS, ALU.mult, ALU.add)\
                    .then_inc(var_ready, 1)
                dve.wait_ge(std_ready, l + 1)
                link(nc.vector.reciprocal(rstd[:, :], std[:, :]))
                link(nc.vector.tensor_tensor(newton[:, :], rstd[:, :], rstd[:, :], ALU.mult))
                link(nc.vector.scalar_tensor_tensor(out=newton[:, :], in0=newton[:, :], scalar=-0.5, in1=var[:, :],
                                                    op0=ALU.mult, op1=ALU.mult))
                link(nc.vector.scalar_tensor_tensor(out=rstd[:, :], in0=newton[:, :], scalar=1.5, in1=rstd[:, :],
                                                    op0=ALU.add, op1=ALU.mult))
                nc.vector.tensor_tensor(diag.rearrange("p (t q) -> p t q", t=4),
                                        ident[:, :].unsqueeze(1).broadcast_to([P, 4, P]),
                                        rstd[:, :].unsqueeze(2).broadcast_to([P, 4, P]), ALU.mult)\
                    .then_inc(diag_ready, 1)

            def modulation(l):
                scale, gate = mod[:, 3 * KD * l + KD:3 * KD * l + 2 * KD], mod[:, 3 * KD * l + 2 * KD:3 * KD * (l + 1)]
                return scale, gate

            def modulated(l):
                scale, _ = modulation(l)
                link(nc.vector.scalar_tensor_tensor(out=gain_mod[:, :], in0=scale, scalar=1.0,
                                                    in1=gain[:, KD * l:KD * (l + 1)], op0=ALU.add, op1=ALU.mult))
                dve.wait_ge(rstd_wide, l + 1)
                shift = 3 * KD * l
                for m in range(KD + 1):
                    if m < KD:
                        if m >= 2:
                            dve.wait_ge(h_hi_ready, KD * l + m - 1)
                            dve.wait_ge(h32_ready, KD * l + m - 1)
                        nc.vector.tensor_tensor(scaled[:, m % 2, :], x[:, m, :], bank[4][:, :], ALU.mult)\
                            .then_inc(scaled_ready, 1)
                    if m:
                        n = m - 1
                        dve.wait_ge(scaled_ready, KD * l + n + 1)
                        if n >= 2:
                            dve.wait_ge(h_ready[n % 2], KD // 2 * l + n // 2)
                        nc.vector.tensor_scalar(h32[:, n % 2, :], scaled[:, n % 2, :], gain_mod[:, n:n + 1],
                                                mod[:, shift + n:shift + n + 1], ALU.mult, ALU.add)\
                            .then_inc(h32_ready, 1)
                        if n % 2 == 0:
                            dve.wait_ge(h32_ready, KD * l + n + 1)
                            dve.wait_ge(h_hi_ready, KD * l + n + 1)
                            nc.vector.tensor_tensor(h_lo[:, n, :], h32[:, n % 2, :], h_hi[:, n, :].bitcast(F32),
                                                    ALU.subtract).then_inc(h_ready[0], 1)

            def mix_split(k):
                split(MIX_CHUNK + k, k % 2, MIX_SIZES[k])

            def mixer():
                def tt(dst, a, b, op):
                    return nc.vector.tensor_tensor(dst, a, b, op)

                def ts(dst, a, s1, s2, op0, op1):
                    return nc.vector.tensor_scalar(dst, a, s1, s2, op0, op1)

                def wide(v, n):
                    return v.unsqueeze(len(v.shape)).broadcast_to([*v.shape, n])

                def rsqrt(n):
                    r, w = mrstd[:, 0:n], mnewton[:, 0:n]
                    link(nc.vector.reciprocal(r, mstd[:, 0:n]))
                    link(tt(w, r, r, ALU.mult))
                    link(tt(w, w, mvar[:, 0:n], ALU.mult))
                    link(ts(w, w, -0.5, 1.5, ALU.mult, ALU.add))
                    link(tt(r, r, w, ALU.mult))

                mix_split(1)
                dve.wait_ge(mixc_in, 32)
                dve.wait_ge(h_ready[0], KD)
                dve.wait_ge(h_ready[1], KD)
                pos, ang, turns = mnewton[:, 0:TOK], angle[2][:, :, :], angle[3][:, :, :]
                link(nc.vector.tensor_copy(pos, pos_int[:, :]))
                link(tt(ang, wide(pos, 16), mixc[:, FREQ_AT:FREQ_AT + 16].unsqueeze(1).broadcast_to([P, TOK, 16]),
                        ALU.mult))
                for fn in range(2):
                    red = angle[fn][:, :, :]
                    link(ts(turns, ang, 1.0 / (2.0 * 3.141592653589793), 0.25 * fn, ALU.mult, ALU.add))
                    link(ts(turns, turns, MAGIC, MAGIC, ALU.add, ALU.subtract))
                    src = ang
                    for part in TWO_PI:
                        link(nc.vector.scalar_tensor_tensor(out=red, in0=turns, scalar=-part, in1=src,
                                                            op0=ALU.mult, op1=ALU.add))
                        src = red
                    if fn:
                        link(ts(red, red, 1.5707963267948966, 3.1415925, ALU.add, ALU.min))
                        nc.vector.tensor_scalar(red, red, -3.1415925, None, ALU.max).then_inc(angle_ready, 1)
                    else:
                        link(ts(red, red, -3.1415925, 3.1415925, ALU.max, ALU.min))
                nc.vector.tensor_scalar(mixc[:, QG_AT:QG_AT + HEAD], mixc[:, QG_AT:QG_AT + HEAD], ATTN_SCALE, None,
                                        ALU.mult).then_inc(mixc_scaled, 1)
                mix_split(2)
                mix_split(3)
                lat_parts = ((0, Q_RANK), (Q_RANK, KV_RANK), (Q_RANK + KV_RANK, ROPE))
                for r in range(2):
                    dve.wait_ge(msq_done, r + 1)
                    for j, (at, n) in enumerate(lat_parts):
                        last = nc.vector.tensor_reduce(mvar[:, TOK * j + 2 * r:TOK * j + 2 * r + 2],
                                                       squares[:, :, at:at + n], AX_X, ALU.add)
                    last.then_inc(msq_used, 1)
                dve.wait_ge(msq_used, 2)
                for j, (at, n) in enumerate(lat_parts):
                    last = ts(mvar[:, TOK * j:TOK * j + TOK], mvar[:, TOK * j:TOK * j + TOK], 1.0 / n, EPS,
                              ALU.mult, ALU.add)
                last.then_inc(mvar_ready, 1)
                dve.wait_ge(mvar_ready, 1)
                dve.wait_ge(mstd_ready, 1)
                rsqrt(3 * TOK)
                for j, (at, n) in enumerate(lat_parts):
                    last = tt(lat[:, :, at:at + n], lat[:, :, at:at + n], wide(mrstd[:, TOK * j:TOK * j + TOK], n),
                              ALU.mult)
                last.then_inc(latn_ready, 1)
                mix_split(4)
                nc.vector.memset(u_pad[:, :, 0:16], 0.0)
                nc.vector.memset(window[0][:, 0:16], 0.0)
                link(nc.vector.memset(window[1][:, 0:16], 0.0))

                def pool(g):
                    dve.wait_ge(u_evac, g + 1)
                    if g >= 1:
                        dve.wait_ge(pooled_lo_done, g)
                    dst = u_pad[:, g, :]
                    src = dst
                    for level in range(g + 1):
                        w = 1 << level
                        dst = window[(g - level) % 2 ^ 1]
                        if level == 0 and g >= 1:
                            link(nc.vector.memset(window[0][:, 0:16], 0.0))
                            link(nc.vector.memset(window[1][:, 0:16], 0.0))
                        link(tt(dst[:, 16:16 + S], src[:, 16:16 + S], src[:, 16 - w:16 + S - w], ALU.add))
                        src = dst
                    link(tt(src[:, 16:32], src[:, 16:32], mixc[:, CORR_AT + 16 * g:CORR_AT + 16 * g + 16], ALU.mult))
                    nc.vector.scalar_tensor_tensor(out=window[g % 2][:, 0:S], in0=src[:, 16:16 + S],
                                                   scalar=1.0 / (2 << g), in1=u_pad[:, g, 16:16 + S],
                                                   op0=ALU.mult, op1=ALU.subtract).then_inc(pooled_ready, 1)

                def pooled_low(g):
                    dve.wait_ge(pooled_hi_done, g + 1)
                    tt(pooled_lo[:, g, :], window[g % 2][:, 0:S], pooled_hi[:, g, :].bitcast(F32),
                       ALU.subtract).then_inc(pooled_lo_done, 1)

                mix_split(5)
                for r in range(Q_TILES + KV_TILES):
                    ft = (r + Q_TILES) % (Q_TILES + KV_TILES)
                    dve.wait_ge(lat_hi_done, r + 1)
                    nc.vector.scalar_tensor_tensor(out=lat_lo[:, ft, :], in0=bank[r][:, :],
                                                   scalar=mixc[:, LG_AT + ft:LG_AT + ft + 1],
                                                   in1=lat_hi[:, ft, :].bitcast(F32), op0=ALU.mult,
                                                   op1=ALU.subtract).then_inc(lat_lo_done, 1)
                mix_split(6)

                def rotate(src, scratch):
                    a, b = scratch
                    c, s = cos[:, :, :], sin[:, :, :]
                    tt(a, src, c, ALU.mult)
                    lo, hi = slice(0, 16), slice(16, 32)
                    tt(b[..., lo], src[..., hi], s[..., lo], ALU.mult)
                    link(tt(b[..., hi], src[..., lo], s[..., hi], ALU.mult))
                    return a, b

                dve.wait_ge(trig_ready, 4)
                dve.wait_ge(latn_ready, 1)
                k_rope = lat[:, :, Q_RANK + KV_RANK:LAT]
                link(tt(k_rope, k_rope, mixc[:, KG_AT + NOPE:KG_AT + HEAD].unsqueeze(1).broadcast_to([P, TOK, ROPE]),
                        ALU.mult))
                a, b = rotate(k_rope, (krot[:, 0], krot[:, 1]))
                for t in range(TOK):
                    tt(qk_tok[:, 1, t, :, NOPE:HEAD], a[:, t, :].unsqueeze(1).broadcast_to([P, HEADS, ROPE]),
                       b[:, t, :].unsqueeze(1).broadcast_to([P, HEADS, ROPE]), ALU.add).then_inc(k_rope_done, 1)
                def head_sums(qk, half, width):
                    n = 2 + 2 * (1 - qk) + half + 1
                    dve.wait_ge(msq_done, n)
                    buf = squares[:, :, 0:HEADS * width].rearrange("p t (h d) -> p t h d", h=HEADS)
                    at = (1 if qk else 0) * TOK * HEADS + 2 * half * HEADS
                    last = nc.vector.tensor_reduce(mvar[:, at:at + 2 * HEADS].rearrange("p (t h) -> p t h", t=2),
                                                   buf[:, :, :, 0:NOPE], AX_X, ALU.add)
                    if qk == 0:
                        at += 2 * TOK * HEADS
                        last = nc.vector.tensor_reduce(mvar[:, at:at + 2 * HEADS].rearrange("p (t h) -> p t h", t=2),
                                                       buf[:, :, :, NOPE:HEAD], AX_X, ALU.add)
                    last.then_inc(msq_used, 1)

                mix_split(7)
                head_sums(1, 0, NOPE)
                head_sums(1, 1, NOPE)
                pool(0)
                pooled_low(0)
                pool(1)
                pooled_low(1)
                pool(2)
                pooled_low(2)
                pool(3)
                pooled_low(3)
                mix_split(8)

                for g in range(POOL_TILES):
                    dve.wait_ge(group_hi_done, g + 1)
                    nc.vector.scalar_tensor_tensor(out=group_lo[:, g, :], in0=bank[(5 + g) % 8][:, :],
                                                   scalar=mixc[:, PS_AT + g:PS_AT + g + 1],
                                                   in1=group_hi[:, g, :].bitcast(F32), op0=ALU.mult,
                                                   op1=ALU.subtract).then_inc(group_lo_done, 1)
                mix_split(9)
                head_sums(0, 0, HEAD)
                head_sums(0, 1, HEAD)
                dve.wait_ge(msq_used, 6)
                n = TOK * HEADS
                ts(mvar[:, 0:2 * n], mvar[:, 0:2 * n], 1.0 / NOPE, EPS, ALU.mult, ALU.add)
                ts(mvar[:, 2 * n:3 * n], mvar[:, 2 * n:3 * n], 1.0 / ROPE, EPS, ALU.mult, ALU.add)\
                    .then_inc(mvar_ready, 1)
                dve.wait_ge(mvar_ready, 2)
                dve.wait_ge(mstd_ready, 2)
                rsqrt(3 * n)

                def heads_of(qk):
                    return qk_tok[:, qk].rearrange("p t h d -> p (t h) d")

                dve.wait_ge(mixc_scaled, 1)
                q, k = heads_of(0), heads_of(1)
                tt(q[:, :, 0:NOPE], q[:, :, 0:NOPE], wide(mrstd[:, 0:n], NOPE), ALU.mult)
                tt(k[:, :, 0:NOPE], k[:, :, 0:NOPE], wide(mrstd[:, n:2 * n], NOPE), ALU.mult)
                link(tt(q[:, :, NOPE:HEAD], q[:, :, NOPE:HEAD], wide(mrstd[:, 2 * n:3 * n], ROPE), ALU.mult))
                mix_split(10)

                def gains_of(at, width):
                    return mixc[:, at:at + width].unsqueeze(1).broadcast_to([P, n, width])

                link(tt(q, q, gains_of(QG_AT, HEAD), ALU.mult))
                tt(k[:, :, 0:NOPE], k[:, :, 0:NOPE], gains_of(KG_AT, NOPE), ALU.mult).then_inc(qk_tok_ready, 1)
                for half in range(2):
                    for t in range(2):
                        tok = 2 * half + t
                        src = qk_tok[:, 0, tok, :, NOPE:HEAD]
                        a, b = rot_a[:, tok], rot_b[:, tok]
                        c, s = (v[:, tok, :].unsqueeze(1).broadcast_to([P, HEADS, ROPE]) for v in (cos, sin))
                        tt(a, src, c, ALU.mult)
                        tt(b[:, :, 0:16], src[:, :, 16:32], s[:, :, 0:16], ALU.mult)
                        link(tt(b[:, :, 16:32], src[:, :, 0:16], s[:, :, 16:32], ALU.mult))
                last = tt(q[:, :, NOPE:HEAD], rot_a[:, :, :, :].rearrange("p t h d -> p (t h) d"),
                          rot_b[:, :, :, :].rearrange("p t h d -> p (t h) d"), ALU.add)
                last.then_inc(qk_tok_ready, 1)
                for h in range(HEADS):
                    dve.wait_ge(qk_t_ready, 2 * h + 2)
                    nc.vector.tensor_copy(k_t[0:HEAD, h, :], bank[(2 + 2 * h) % 8][0:HEAD, :]).then_inc(k_t_evac, 1)

                def head(i, s, half):
                    h = HEADS // 2 * half + 2 * i + s
                    for qt in range(TOK):
                        dve.wait_ge(scores_ready, TOK * h + qt + 1)
                        nc.vector.tensor_reduce(row_max[:, qt:qt + 1], bank[qt][:, 0:(qt + 1) * P], AX_X, ALU.max,
                                                negate=True).then_inc(max_ready, 1)

                    def gate(g):
                        if not half:
                            dve.wait_ge(tanh_done, 2 * h + g + 1)
                            part = br_pool[:, bass.ds(2 * (2 * i + s) + g, 1), :].rearrange("p a s -> p (a s)")
                            nc.vector.scalar_tensor_tensor(out=part, in0=scaled[:, g, :], scalar=1.0, in1=part,
                                                           op0=ALU.add, op1=ALU.mult).then_inc(gated, 1)

                    split(MIX_CHUNK + GATE_AT + h + 1, 1 - s, SLOT)
                    dve.wait_ge(p_ready, TOK * h + TOK)
                    nc.vector.reciprocal(row_inv[:, :], row_sum[:, :]).then_inc(inv_done, 1)
                    dve.wait_ge(p_t_ready, 3 * h + 1)
                    nc.vector.tensor_copy(p_t[:, 0:4, :].rearrange("p b q -> p (b q)"), bank[0][:, :])\
                        .then_inc(p_t_dve, 1)
                    dve.wait_ge(p_t_ready, 3 * h + 3)
                    nc.vector.tensor_copy(p_t[:, 8:10, :].rearrange("p b q -> p (b q)"), bank[2][:, 0:2 * P])\
                        .then_inc(p_t_dve, 1)
                    gate(0)
                    dve.wait_ge(inv_done, h + 1)
                    dve.wait_ge(pv_ready, h + 1)
                    nc.vector.tensor_tensor(attn_tok[:, :, bass.ds(V_DIM * h, V_DIM)],
                                            bank[6][:, 0:TOK * V_DIM].rearrange("p (t d) -> p t d", t=TOK),
                                            wide(row_inv[:, :], V_DIM), ALU.mult).then_inc(pv_evac, 1)
                    gate(1)

                for half in range(2):
                    with dve.Fori(0, HEADS // 4) as i:
                        for s in range(2):
                            head(i, s, half)
                for f in range(4):
                    dve.wait_ge(attn_hi_done, f + 1)
                    tt(attn_lo[:, f, :], bank[f][:, :], attn_hi[:, f, :].bitcast(F32), ALU.subtract)\
                        .then_inc(attn_lo_done, 1)
                _, gate_cols = modulation(1)
                link(nc.vector.tensor_scalar(out_gate[:, :], gate_cols, 0.5, None, ALU.mult))
                def merged_low(m):
                    dve.wait_ge(merged_hi_done, m + 1)
                    tt(h_lo[:, m, :], h32[:, m % 2, :], h_hi[:, m, :].bitcast(F32), ALU.subtract)\
                        .then_inc(merged_lo_done, 1)

                for m in range(KD):
                    if m % 4 == 0:
                        mix_split(19 + m // 4)
                    dve.wait_ge(mla_ready, m + 1)
                    dve.wait_ge(tanh_done, 2 * HEADS)
                    nc.vector.scalar_tensor_tensor(out=tanh_mla[:, m, :], in0=tanh_mla[:, m, :], scalar=1.0,
                                                   in1=bank[(4 + m) % 8][:, :], op0=ALU.add, op1=ALU.mult)\
                        .then_inc(mla_gated, 1)
                    if m:
                        merged_low(m - 1)
                merged_low(KD - 1)
                for c in range(4):
                    if c < 3:
                        mix_split(21 + c)
                    else:
                        split(FIRST_CHUNK[1], 0, IN_ELEMS)
                    for g in range(2):
                        m = 2 * c + g
                        dve.wait_ge(pe_used, FFN_CHUNKS + c + 1)
                        nc.vector.scalar_tensor_tensor(out=x[:, m, :], in0=bank[4 + m % 4][:, :],
                                                       scalar=out_gate[:, m:m + 1], in1=x[:, m, :],
                                                       op0=ALU.mult, op1=ALU.add).then_inc(out_evac, 1)

            def ffn(f, after):
                n0, u0 = FIRST_CHUNK[f], FFN_USED[f]

                def up(i, first, last):
                    for s in range(2):
                        j = 2 * i + s
                        split(n0 + j + 1, 1 - s, OUT_ELEMS if last and s else IN_ELEMS)
                        if f == 0:
                            add_ada(ADA_START + i, range(4 * s, 4 * s + 4))
                        if not (f == 0 and first and s == 0):
                            dve.wait_ge(act_done, NF * f + j)
                        dve.wait_ge(silu_done, NF * f + j + 1)
                        nc.vector.tensor_tensor(prod, silu_g, bank[2 * s + 1][:, :], ALU.mult).then_inc(gu_evac, 1)
                        dve.wait_ge(act_hi_done, NF * f + j + 1)
                        nc.vector.tensor_tensor(act_lo[f][:, bass.ds(j, 1), :], prod.unsqueeze(1),
                                                act_hi[f][:, bass.ds(j, 1), :].bitcast(F32), ALU.subtract)\
                            .then_inc(act_done, 1)
                        if f == 0 and s == 0 and not first:
                            keep_mod(ADA_START + i - 1)

                up(0, True, False)
                with dve.Fori(1, NFH - 1) as i:
                    up(i, False, False)
                up(NFH - 1, False, True)
                _, gate = modulation(2 * f)
                link(nc.vector.tensor_scalar(out_gate[:, :], gate, 0.5, None, ALU.mult))

                def down(i, last):
                    for s in range(4):
                        q = NF + 4 * i + s
                        if not (last and s == 3):
                            split(n0 + q + 1, (s + 1) % 2, OUT_ELEMS)
                        elif after:
                            after()
                        if f == 0 and s == 0:
                            keep_mod(ADA_START + NFH + i - 1)
                        if f == 0 and not last and s % 2 == 0:
                            add_ada(ADA_START + NFH + i, range(2 * s, 2 * s + 4))
                        if s % 2:
                            m = 2 * i + s // 2
                            dve.wait_ge(pe_used, u0 + q + 1)
                            xm = x[:, bass.ds(m, 1), :]
                            nc.vector.scalar_tensor_tensor(out=xm, in0=bank[4 + s // 2][:, :].unsqueeze(1),
                                                           scalar=out_gate[:, bass.ds(m, 1)], in1=xm,
                                                           op0=ALU.mult, op1=ALU.add).then_inc(out_evac, 1)

                with dve.Fori(0, 3) as i:
                    down(i, False)
                down(3, True)

            nc.vector.memset(ones[:, :], 1.0).then_inc(ones_ready, 1)
            nc.vector.memset(rstd[:, :], 0.0).then_inc(gu_evac, 2)
            nc.vector.memset(newton[:, :], 0.0).then_inc(out_evac, 2)
            dve.wait_ge(const_in, 64)
            norm(0)
            for g in range(ADA_START):
                keep_mod(g)
            dve.wait_ge(mod_ready, ADA_START)
            modulated(0)
            split(0, 0, IN_ELEMS)
            ffn(0, lambda: mix_split(0))
            norm(1)
            modulated(1)
            mixer()
            norm(2)
            modulated(2)
            ffn(1, None)

        @block.gpsimd
        def _(pool):
            def squares_up(l):
                pool.wait_ge(sq_done, KD * l + 1)
                nc.gpsimd.tensor_copy(ssq[:, :], square).then_inc(sq_added, 1)
                with pool.Fori(1, KD - 1) as m:
                    pool.wait_ge(sq_done, m + (KD * l + 1))
                    pool.wait_ge(sq_added, m + (KD - 1) * l)
                    nc.gpsimd.tensor_tensor(ssq[:, :], ssq[:, :], square, ALU.add).then_inc(sq_added, 1)

            def norm(l):
                for m in range(1, KD, 2):
                    pool.wait_ge(h32_ready, KD * l + m + 1)
                    pool.wait_ge(h_hi_ready, KD * l + m + 1)
                    nc.gpsimd.tensor_tensor(h_lo[:, m, :], h32[:, m % 2, :], h_hi[:, m, :].bitcast(F32),
                                            ALU.subtract).then_inc(h_ready[1], 1)

            squares_up(0)
            norm(0)
            squares_up(1)
            norm(1)
            pool.wait_ge(gated, KD)
            for m in range(KD):
                pool.wait_ge(mla_gated, m + 1)
                if m >= 2:
                    pool.wait_ge(merged_lo_done, m - 1)
                nc.gpsimd.tensor_tensor(h32[:, m % 2, :], tanh_mla[:, m, :], br_pool[:, m, :], ALU.add)\
                    .then_inc(merged_ready, 1)
            squares_up(2)
            norm(2)


def kernel(x, c, positions, w_ada, b_ada, norm_ffn1, w_ffn1_in, w_ffn1_out,
           norm_mix, w_in, pool_grp, pool_scale, w_pool_proj, q_a_norm, w_q_up,
           kv_a_norm, w_kv_up, q_norm_nope, q_norm_rope, k_norm_nope, k_norm_rope,
           w_mla_proj, w_out, norm_ffn2, w_ffn2_in, w_ffn2_out):
    import numpy as np
    import concourse.bacc as bacc
    from concourse.bass_utils import run_bass_kernel_spmd

    def cols(v):
        return np.asarray(v).reshape(-1, P).T

    ffn_in = [np.asarray(w)[0].reshape(KD, P, 2, NF, P).transpose(3, 1, 2, 0, 4).reshape(NF, P, IN_ELEMS)
              for w in (w_ffn1_in, w_ffn2_in)]
    ffn_out = [np.asarray(w)[0].reshape(2, NFH, P, KD, P).transpose(3, 0, 2, 1, 4).reshape(2 * KD, P, OUT_ELEMS)
               for w in (w_ffn1_out, w_ffn2_out)]
    w = np.asarray(w_in)[0]
    at = np.cumsum([0, 512, LAT, D, D])
    kv = np.asarray(w_kv_up)[0].reshape(KV_TILES, P, HEADS, 2, NOPE).transpose(1, 0, 3, 2, 4).reshape(P, -1)
    q_up = np.asarray(w_q_up)[0].reshape(Q_TILES, P, 2, 384).transpose(2, 1, 0, 3).reshape(2, P, -1)
    grp = np.asarray(pool_grp)[0].transpose(1, 0, 2).reshape(P, -1)

    def tiles(m, per_chunk):
        kt, mt = m.shape[0] // P, m.shape[1] // P
        return list(m.reshape(kt, P, mt // per_chunk, per_chunk, P).transpose(2, 1, 3, 0, 4)
                    .reshape(mt // per_chunk, P, per_chunk * kt * P))

    mix = [w[:, 512 + a:512 + a + n].reshape(KD, P, n).transpose(1, 0, 2).reshape(P, -1) for a, n in LAT_COLS]
    mix += tiles(w[:, 0:512], 2) + [kv, q_up[0], np.concatenate([q_up[1], grp], axis=1)]
    mix += tiles(np.asarray(w_pool_proj)[0], 4) + tiles(w[:, at[2]:at[4]], 2)
    mix += tiles(np.asarray(w_mla_proj)[0], 4) + tiles(np.asarray(w_out)[0], 2)
    w_mix = np.zeros((len(mix), P, SLOT), np.float32)
    for n, m in enumerate(mix):
        assert m.shape[1] == MIX_SIZES[n]
        w_mix[n, :, 0:m.shape[1]] = m
    tok = np.arange(P)
    mask = np.where(tok[None, :] <= tok[:, None], np.float32(0), np.float32(-1e30))
    first = np.arange(1, 17)
    corr = np.concatenate([(2 << g) / np.minimum(first, 2 << g) for g in range(POOL_TILES)])
    freq = np.float32(10000.0) ** (-np.arange(0, ROPE, 2, dtype=np.float32) / np.float32(ROPE))
    rows = [np.asarray(v)[0] for v in (q_norm_nope, q_norm_rope, k_norm_nope, k_norm_rope)]
    mix_consts = np.concatenate(
        [mask] + [np.broadcast_to(v.astype(np.float32), (P, len(v))) for v in (*rows, corr, freq)]
        + [cols(v[0]) for v in (q_a_norm, kv_a_norm, pool_scale)], axis=1)
    arrays = {
        "x_t": np.asarray(x)[0].T.reshape(KD, P, S).transpose(1, 0, 2),
        "c_t": cols(c[0]),
        "gains": np.concatenate([cols(g[0]) for g in (norm_ffn1, norm_mix, norm_ffn2)], axis=1),
        "b_ada": cols(b_ada[0]),
        "w_ada": np.asarray(w_ada)[0].reshape(KD, P, ADA_GROUPS, ADA_COLS).transpose(2, 0, 1, 3),
        "w_ffn_in": np.stack(ffn_in),
        "w_ffn_out": np.stack(ffn_out),
        "w_mix": w_mix,
        "mix_consts": mix_consts,
        "positions": np.asarray(positions)[0].reshape(TOK, P).T,
        "consts": np.eye(P, dtype=np.float32),
    }
    arrays = {n: np.ascontiguousarray(a) for n, a in arrays.items()}
    nc = bacc.Bacc("TRN2", target_bir_lowering=False, num_devices=1)
    args = [nc.dram_tensor(n, a.shape, mybir.dt.from_np(a.dtype), kind="ExternalInput").ap() for n, a in arrays.items()]
    out = nc.dram_tensor("out", (KD, P, S), F32, kind="ExternalOutput").ap()
    program(nc, *args, out)
    got = run_bass_kernel_spmd(nc, [arrays], core_ids=[0]).results[0]["out"]
    return np.ascontiguousarray(got.reshape(D, S).T)[None]
```

```python
from contextlib import ExitStack

import concourse.bass as bass
from concourse import mybir

ALU = mybir.AluOpType
ACT = mybir.ActivationFunctionType
F32 = mybir.dt.float32
F32R = mybir.dt.float32r
AX_X = mybir.AxisListType.X

P = 128
D = 1024
S = 512
D_FF = 2816
EPS = 1e-6
KD = D // P
NF = D_FF // P
NFH = NF // 2
IN_ELEMS = 2 * KD * P
OUT_ELEMS = NFH * P
ADA_COLS = 512
ADA_GROUPS = 9 * D // ADA_COLS
ADA_START = 2 * D // ADA_COLS
FIRST_GROUPS = [0, 2, 1, 3]
FFN_CHUNKS = NF + 2 * KD
FIRST_CHUNK = [0, FFN_CHUNKS + 24]
FFN_USED = [0, FFN_CHUNKS + 4]
SLOT = 2048

HEADS = 8
NOPE = 64
ROPE = 32
HEAD = NOPE + ROPE
V_DIM = 64
Q_RANK = 384
KV_RANK = 256
LAT = Q_RANK + KV_RANK + ROPE
Q_TILES = Q_RANK // P
KV_TILES = KV_RANK // P
POOL_TILES = 4
TOK = S // P
ATTN_SCALE = 1.0 / HEAD ** 0.5
LAT_COLS = [(0, 256), (256, 256), (512, 160)]
MIX_CHUNK = FFN_CHUNKS
MIX_SIZES = [KD * n for _, n in LAT_COLS] + [SLOT, SLOT, KV_TILES * 1024, Q_TILES * 384, Q_TILES * 384 + 4 * P,
                                             SLOT, SLOT] + [SLOT] * 8 + [SLOT] * 2 + [SLOT] * 4
LAT_AT, UPOOL_AT, KV_AT, Q_AT, PP_AT, GATE_AT, MLA_AT, WOUT_AT = 0, 3, 5, 6, 8, 10, 18, 20
MASK_AT, QG_AT, KG_AT = 0, P, P + HEAD
CORR_AT = KG_AT + HEAD
FREQ_AT = CORR_AT + 16 * POOL_TILES
LG_AT = FREQ_AT + ROPE // 2
PS_AT = LG_AT + Q_TILES + KV_TILES
MIXC = PS_AT + POOL_TILES
TWO_PI = (6.28125, 0.0019350051879882812, 3.0199159819567e-07)
P_PARTS = [(0, 4), (4, 4), (8, 2)]
P_BLOCKS = [(qt, kt) for kt in range(TOK) for qt in range(kt, TOK)]
MAGIC = 1.5 * 2.0 ** 23


def program(nc, x_t, c_t, gains, b_ada, w_ada, w_ffn_in, w_ffn_out, w_mix, mix_consts, positions, consts, out):
    ctx = ExitStack()
    with ctx:
        cursor = [16512]

        def place(name, shape, dt=F32, at=None):
            size = 4
            for n in shape[1:]:
                size *= n
            if at is None:
                at = cursor[0]
                cursor[0] += (size + 31) // 32 * 32
            assert at + size <= 229344, (name, at + size)
            return nc.alloc_sbuf_tensor_at(name, shape, dt, offset=at)

        def sem(name):
            return ctx.enter_context(nc.semaphore(name))

        x = place("x", [P, KD, S])
        h_hi = place("h_hi", [P, KD, S], F32R)
        h_lo = place("h_lo", [P, KD, S], F32R)
        w_raw = [place(f"w_raw{i}", [P, SLOT]) for i in range(2)]
        w_hi = [place(f"w_hi{i}", [P, SLOT], F32R) for i in range(2)]
        w_lo = [place(f"w_lo{i}", [P, SLOT], F32R) for i in range(2)]
        ident = place("ident", [P, P])
        ones = place("ones", [P, P])
        mod = place("mod", [P, 72])
        bias_ada = place("bias_ada", [P, 72])
        gain = place("gain", [P, 3 * KD])
        c_raw = place("c_raw", [P, KD])
        c_act = place("c_act", [P, KD])
        gain_mod = place("gain_mod", [P, KD])
        out_gate = place("out_gate", [P, KD])
        var = place("var", [P, 4])
        std = place("std", [P, 4])
        rstd = place("rstd", [P, 4])
        newton = place("newton", [P, 4])
        warm = place("warm", [P, 8])
        pool_note = place("pool_note", [P, 1])
        ones_r = place("ones_r", [P, 2], F32R)
        scaled_at = cursor[0]
        scaled = place("scaled", [P, 2, S])
        h32 = place("h32", [P, 2, S])
        ssq = place("ssq", [P, S])
        ada_acc = place("ada_acc", [P, ADA_COLS])
        phase_at = cursor[0]
        silu_g = scaled[:, 0, :]
        prod = scaled[:, 1, :]
        square = scaled[:, 0, :]
        diag = scaled[:, 1, :]
        acc_hi = place("acc_hi", [P, ADA_COLS], F32R, at=scaled_at + 4096)
        acc_lo = place("acc_lo", [P, ADA_COLS], F32R, at=scaled_at + 4096 + 4 * ADA_COLS)

        ada_raw = place("ada_raw", [P, KD // 2, ADA_COLS], at=phase_at)
        act_at = phase_at + 4 * 4 * ADA_COLS
        ada_first = place("ada_first", [P, ADA_START, KD, ADA_COLS], at=act_at)
        first_at = act_at + 4 * ADA_START * KD * ADA_COLS + 4 * KD * S
        first_acc = place("first_acc", [P, ADA_COLS], at=first_at)
        first_hi = place("first_hi", [P, ADA_COLS], F32R, at=first_at + 4 * ADA_COLS)
        first_lo = place("first_lo", [P, ADA_COLS], F32R, at=first_at + 8 * ADA_COLS)
        sums_of = ((ada_acc, acc_hi, acc_lo), (first_acc, first_hi, first_lo))
        act_hi = [place(f"act_hi{f}", [P, NF, S], F32R, at=act_at) for f in range(2)]
        act_lo = [place(f"act_lo{f}", [P, NF, S], F32R, at=act_at + 4 * NF * S) for f in range(2)]

        kib = 1024
        v_tok = place("v_tok", [P, TOK, HEADS * V_DIM], at=phase_at)
        br_pool = place("br_pool", [P, KD, S], at=phase_at + 8 * kib)
        u_pad = place("u_pad", [P, POOL_TILES, 16 + S], at=phase_at + 8 * kib)
        window = [place(f"window{i}", [P, 16 + S], at=phase_at + 8 * kib + 4 * (POOL_TILES + i) * (16 + S))
                  for i in range(2)]
        lat = place("lat", [P, TOK, LAT], at=phase_at + 24 * kib)
        lat_hi = place("lat_hi", [P, Q_TILES + KV_TILES, S], F32R, at=phase_at + 24 * kib + 4 * TOK * LAT)
        lat_lo = place("lat_lo", [P, Q_TILES + KV_TILES, S], F32R, at=phase_at + 34 * kib + 4 * TOK * LAT)
        group_hi = place("group_hi", [P, POOL_TILES, S], F32R, at=phase_at + 24 * kib)
        group_lo = place("group_lo", [P, POOL_TILES, S], F32R, at=phase_at + 32 * kib)
        q_t = place("q_t", [P, HEADS, S], at=phase_at + 24 * kib)
        k_t = place("k_t", [P, HEADS, S], at=phase_at + 40 * kib)
        attn_hi = place("attn_hi", [P, 4, S], F32R, at=phase_at + 24 * kib)
        attn_lo = place("attn_lo", [P, 4, S], F32R, at=phase_at + 40 * kib)
        qk_tok = place("qk_tok", [P, 2, TOK, HEADS, HEAD], at=phase_at + 56 * kib)
        p_tok = place("p_tok", [P, 10, P], at=phase_at + 64 * kib)
        p_hi = place("p_hi", [P, 10, P], F32R, at=phase_at + 69 * kib)
        p_lo = place("p_lo", [P, 10, P], F32R, at=phase_at + 74 * kib)
        q_now = place("q_now", [P, S], at=scaled_at + 6144)
        pooled_hi = place("pooled_hi", [P, POOL_TILES, S], F32R, at=phase_at + 80 * kib)
        pooled_lo = place("pooled_lo", [P, POOL_TILES, S], F32R, at=phase_at + 88 * kib)
        tanh_mla = place("tanh_mla", [P, KD, S], at=phase_at + 80 * kib)
        mixc = place("mixc", [P, MIXC], at=cursor[0] - 4096)
        cursor[0] = (cursor[0] - 4096 + 4 * MIXC + 31) // 32 * 32
        small_end = cursor[0]
        pos_int = place("pos_int", [P, TOK], mybir.dt.int32)
        cos = place("cos", [P, TOK, ROPE])
        sin = place("sin", [P, TOK, ROPE])
        mvar = place("mvar", [P, 3 * TOK * HEADS])
        mstd = place("mstd", [P, 3 * TOK * HEADS])
        mrstd = place("mrstd", [P, 3 * TOK * HEADS])
        mnewton = place("mnewton", [P, 3 * TOK * HEADS], at=scaled_at + 7168)
        assert cursor[0] <= phase_at, cursor[0] - phase_at
        spare = [96 * kib + phase_at]

        def place_small(name, shape, dt=F32):
            t = place(name, shape, dt, at=spare[0])
            spare[0] += 32
            return t

        row_max = place_small("row_max", [P, TOK])
        row_sum = place_small("row_sum", [P, TOK])
        row_inv = place_small("row_inv", [P, TOK])
        squares = place("squares", [P, 2, HEADS * HEAD], at=scaled_at)
        rot_a = place("rot_a", [P, TOK, HEADS, ROPE], at=scaled_at)
        rot_b = place("rot_b", [P, TOK, HEADS, ROPE], at=scaled_at + 4096)
        krot = place("krot", [P, 2, TOK, ROPE], at=scaled_at + 6144)
        angle = [place(f"angle{i}", [P, TOK, ROPE // 2], at=scaled_at + 6144 + 256 * i) for i in range(4)]

        sq_first = place("sq_first", [P, KD, S], at=act_at + 4 * ADA_START * KD * ADA_COLS)
        mask_r = place("mask_r", [P, P], F32R, at=phase_at + 79 * kib)
        ident_r = place("ident_r", [P, P], F32R, at=phase_at + 79 * kib + 4 * P)
        v_hi = place("v_hi", [P, TOK, 3 * V_DIM], F32R, at=phase_at + 56 * kib)
        v_lo = place("v_lo", [P, TOK, 3 * V_DIM], F32R, at=phase_at + 60 * kib)

        bank = [ctx.enter_context(nc.psum_tensor(f"bank{i}", [P, S], F32)) for i in range(8)]
        ADA_BANK, STAT_BANK = bank[6], bank[7]

        const_in = sem("const_in")
        c_in = sem("c_in")
        first_step = [sem(f"first_step{n}") for n in range(ADA_START)]
        x_in = sem("x_in")
        raw_in = [sem(f"raw_in{i}") for i in range(2)]
        ada_first_in = [sem(f"ada_first_in{i}") for i in range(2 * ADA_START)]
        ada_in = [sem(f"ada_in{i}") for i in range(4)]
        hi_done = sem("hi_done")
        lo_done = sem("lo_done")
        pe_used = sem("pe_used")
        c_ready = sem("c_ready")
        ones_ready = sem("ones_ready")
        ada_step = sem("ada_step")
        ada_summed = sem("ada_summed")
        mod_ready = sem("mod_ready")
        sq_done = sem("sq_done")
        sq_added = sem("sq_added")
        ssq_ready = sem("ssq_ready")
        stat_ready = sem("stat_ready")
        var_ready = sem("var_ready")
        std_ready = sem("std_ready")
        small = sem("small")
        diag_ready = sem("diag_ready")
        rstd_wide = sem("rstd_wide")
        scaled_ready = sem("scaled_ready")
        h32_ready = sem("h32_ready")
        h_hi_ready = sem("h_hi_ready")
        h_ready = [sem("h_ready_even"), sem("h_ready_odd")]
        gu_ready = sem("gu_ready")
        silu_done = sem("silu_done")
        gu_evac = sem("gu_evac")
        act_hi_done = sem("act_hi_done")
        act_done = sem("act_done")
        out_ready = sem("out_ready")
        out_evac = sem("out_evac")
        stored = sem("stored")

        mixc_in = sem("mixc_in")
        mixc_scaled = sem("mixc_scaled")
        lat_ready = sem("lat_ready")
        lat_evac = sem("lat_evac")
        u_ready = sem("u_ready")
        u_evac = sem("u_evac")
        msq_done = sem("msq_done")
        msq_used = sem("msq_used")
        mvar_ready = sem("mvar_ready")
        mstd_ready = sem("mstd_ready")
        latn_ready = sem("latn_ready")
        lat_t_ready = sem("lat_t_ready")
        lat_hi_done = sem("lat_hi_done")
        lat_lo_done = sem("lat_lo_done")
        angle_ready = sem("angle_ready")
        trig_ready = sem("trig_ready")
        kv_ready = sem("kv_ready")
        kv_evac = sem("kv_evac")
        q_ready = sem("q_ready")
        q_evac = sem("q_evac")
        pooled_ready = sem("pooled_ready")
        pooled_hi_done = sem("pooled_hi_done")
        pooled_lo_done = sem("pooled_lo_done")
        group_ready = sem("group_ready")
        group_hi_done = sem("group_hi_done")
        group_lo_done = sem("group_lo_done")
        proj_ready = sem("proj_ready")
        proj_evac = sem("proj_evac")
        qk_tok_ready = sem("qk_tok_ready")
        qk_t_ready = sem("qk_t_ready")
        q_t_evac = sem("q_t_evac")
        k_t_evac = sem("k_t_evac")
        q_now_ready = sem("q_now_ready")
        scores_ready = sem("scores_ready")
        max_ready = sem("max_ready")
        p_ready = sem("p_ready")
        p_t_ready = sem("p_t_ready")
        p_lo_done = sem("p_lo_done")
        gate_ready = sem("gate_ready")
        tanh_done = sem("tanh_done")
        pv_ready = sem("pv_ready")
        v_zero = sem("v_zero")
        attn_hi_done = sem("attn_hi_done")
        attn_taken = sem("attn_taken")
        mla_ready = sem("mla_ready")
        merged_ready = sem("merged_ready")
        merged_hi_done = sem("merged_hi_done")
        merged_lo_done = sem("merged_lo_done")
        acc_hi_done = sem("acc_hi_done")
        acc_lo_done = sem("acc_lo_done")
        ones_r_ready = sem("ones_r_ready")
        pool_chain = sem("pool_chain")
        mask_ready = sem("mask_ready")
        v_hi_done = sem("v_hi_done")
        v_lo_done = sem("v_lo_done")
        p_hi_done = sem("p_hi_done")
        k_stat_ready = sem("k_stat_ready")
        k_scaled = sem("k_scaled")
        gated = sem("gated")
        mla_gated = sem("mla_gated")
        inv_done = sem("inv_done")
        p_scaled = sem("p_scaled")
        k_rope_done = sem("k_rope_done")

        block = ctx.enter_context(nc.Block())

        chunk_used = ([(lat_ready, TOK * (c + 1)) for c in range(3)] + [(u_ready, 2 * c + 2) for c in range(2)]
                      + [(kv_ready, 8), (q_ready, 4), (group_ready, 4)] + [(proj_ready, 4 * c + 4) for c in range(2)]
                      + [(gate_ready, 2 * c + 2) for c in range(HEADS)] + [(mla_ready, 4 * c + 4) for c in range(2)]
                      + [(pe_used, FFN_CHUNKS + c + 1) for c in range(4)])

        @block.sync
        def _(sp):
            def load_w(src, slot, size, lo_count):
                if lo_count is not None:
                    sp.wait_ge(lo_done, lo_count)
                sp.dma_start(w_raw[slot][:, 0:size], src).then_inc(raw_in[slot], 16)

            def load_ada(group, kt, wait=True):
                if wait:
                    sp.wait_ge(ada_step, 8 * (group - ADA_START) + kt - 3)
                sp.dma_start(ada_raw[:, kt % 4, :], w_ada[group, kt]).then_inc(ada_in[kt % 4], 16)

            def half_ada(group, s):
                for kt in range(4):
                    load_ada(group + s, 4 - 4 * s + kt)

            def ffn(f, after):
                n0 = FIRST_CHUNK[f]

                def up(i, last):
                    for s in range(2):
                        j = 2 * i + s
                        if last:
                            load_w(w_ffn_out[f, s], s, OUT_ELEMS, n0 + j + 1)
                        else:
                            load_w(w_ffn_in[f, j + 2], s, IN_ELEMS, n0 + j + 1)
                        if f == 0:
                            half_ada(ADA_START + i, s)

                with sp.Fori(0, NFH - 1) as i:
                    up(i, False)
                up(NFH - 1, True)

                def down(i, ada, last):
                    for s in range(4):
                        q = 4 * i + s
                        if last and s >= 2:
                            if after:
                                after(s - 2)
                        else:
                            load_w(w_ffn_out[f, q + 2], s % 2, OUT_ELEMS, n0 + NF + q + 1)
                        if ada and s in ada:
                            half_ada(ADA_START + NFH + i, s // 2)

                with sp.Fori(0, 2) as i:
                    down(i, (0, 2) if f == 0 else None, False)
                down(2, (0,) if f == 0 else None, False)
                down(3, None, True)

            def first_ada(n, half):
                g, kts = FIRST_GROUPS[n], slice(4 * half, 4 * half + 4)
                sp.dma_start(ada_first[:, g, kts, :], w_ada[g, kts].rearrange("k p c -> p k c"))\
                    .then_inc(ada_first_in[2 * n + half], 16)

            sp.dma_start(c_raw[:, :], c_t).then_inc(c_in, 16)
            first_ada(0, 0)
            first_ada(1, 0)
            sp.dma_start(x[:, :, :], x_t).then_inc(x_in, 16)
            sp.dma_start(gain[:, :], gains).then_inc(const_in, 16)
            sp.dma_start(bias_ada[:, :], b_ada).then_inc(const_in, 16)
            sp.dma_start(ident[:, :], consts[:, 0:P]).then_inc(const_in, 16)
            first_ada(0, 1)
            first_ada(1, 1)
            first_ada(2, 0)
            first_ada(3, 0)
            load_w(w_ffn_in[0, 0], 0, IN_ELEMS, None)
            first_ada(2, 1)
            first_ada(3, 1)
            load_w(w_ffn_in[0, 1], 1, IN_ELEMS, None)
            for kt in range(4):
                load_ada(ADA_START, kt, False)
            def mix_w(k):
                load_w(w_mix[k, :, 0:MIX_SIZES[k]], k % 2, MIX_SIZES[k], MIX_CHUNK + k - 1)

            ffn(0, mix_w)
            sp.wait_ge(stat_ready, 2)
            sp.dma_start(mixc[:, :], mix_consts).then_inc(mixc_in, 16)
            sp.dma_start(pos_int[:, :], positions).then_inc(mixc_in, 16)
            for k in range(2, GATE_AT):
                mix_w(k)
            with sp.Fori(GATE_AT // 2, len(MIX_SIZES) // 2) as i:
                for s in range(2):
                    load_w(w_mix[2 * i + s], s, SLOT, MIX_CHUNK + 2 * i + s - 1)
            for s in range(2):
                load_w(w_ffn_in[1, s], s, IN_ELEMS, FIRST_CHUNK[1] + s - 1)
            ffn(1, None)
            with sp.Fori(0, KD) as m:
                sp.wait_ge(out_evac, 2 * KD + m + 3)
                sp.dma_start(out[m], x[:, bass.ds(m, 1), :].rearrange("p a s -> p (a s)")).then_inc(stored, 16)
            sp.wait_ge(stored, 16 * KD)

        @block.tensor
        def _(pe):
            def product(dst, stationary, moving, start, stop):
                (a_hi, a_lo), (b_hi, b_lo) = stationary, moving
                nc.tensor.matmul(dst, a_hi, b_hi, start=start, stop=False)
                nc.tensor.matmul(dst, a_lo, b_hi, start=False, stop=False)
                return nc.tensor.matmul(dst, a_hi, b_lo, start=False, stop=stop)

            def w_tile(slot, t):
                cols = slice(t * P, (t + 1) * P)
                return w_hi[slot][:, cols], w_lo[slot][:, cols]

            def reduce_first(n):
                pe.wait_ge(acc_lo_done, n + 1)
                if n >= 2:
                    pe.wait_ge(mod_ready, n // 2 * 2)
                reduce_to(FIRST_GROUPS[n], n % 2)

            def reduce_ada(group):
                pe.wait_ge(acc_lo_done, group + 1)
                pe.wait_ge(mod_ready, group)
                reduce_to(group, 0)

            def reduce_to(group, buf):
                _, hi, lo = sums_of[buf]
                for c in range(4):
                    dst, cols = ADA_BANK[:, bass.ds(8 * group + 2 * c, 2)], slice(c * P, (c + 1) * P)
                    nc.tensor.matmul(dst, hi[:, cols], ones_r[:, :], start=True, stop=False)
                    last = nc.tensor.matmul(dst, lo[:, cols], ones_r[:, :], start=False, stop=True)
                last.then_inc(ada_summed, 1)

            def norm(l):
                pe.wait_ge(ssq_ready, l + 1)
                for t in range(4):
                    last = nc.tensor.matmul(STAT_BANK[:, t:t + 1], ssq[:, t * P:(t + 1) * P], ones[:, 0:1],
                                            start=True, stop=True)
                last.then_inc(stat_ready, 1)

            def norm_wide(l):
                pe.wait_ge(diag_ready, l + 1)
                nc.tensor.matmul(bank[4][:, :], ones[:, :], diag, start=True, stop=True).then_inc(rstd_wide, 1)

            def ffn(f):
                n0 = FIRST_CHUNK[f]

                def up(i, first):
                    for s in range(2):
                        j = 2 * i + s
                        pe.wait_ge(lo_done, n0 + j + 1)
                        pe.wait_ge(gu_evac, NF * f + j + 1)
                        for k in range(KD):
                            if first and s == 0:
                                pe.wait_ge(h_ready[k % 2], KD * f + k // 2 + 1)
                            if f == 0 and not first and s == 0 and k == KD // 2:
                                reduce_ada(ADA_START + i - 1)
                            for gu in range(2):
                                last = product(bank[2 * s + gu][:, :], w_tile(s, gu * KD + k),
                                               (h_hi[:, k, :], h_lo[:, k, :]), k == 0, k == KD - 1)
                        last.then_inc(pe_used, 1)

                up(0, True)
                with pe.Fori(1, NFH) as i:
                    up(i, False)

                def down(i):
                    for mm in range(2):
                        m = 2 * i + mm
                        pe.wait_ge(out_evac, KD * 2 * f + m + 1)
                        for half in range(2):
                            pe.wait_ge(lo_done, n0 + NF + 2 * m + half + 1)
                            pe.wait_ge(act_done, NF * f + NFH * (half + 1))
                            for k in range(NFH):
                                last = product(bank[4 + mm][:, :], w_tile(half, k),
                                               (act_hi[f][:, half * NFH + k, :], act_lo[f][:, half * NFH + k, :]),
                                               half + k == 0, half * k == NFH - 1)
                            last.then_inc(pe_used, 1)
                            if f == 0 and mm == 0 and half == 0:
                                reduce_ada(ADA_START + NFH + i - 1)

                with pe.Fori(0, 4) as i:
                    down(i)

            def h_pair(k, cols=slice(0, S)):
                return h_hi[:, k, cols], h_lo[:, k, cols]

            def toks(t):
                return slice(t * P, (t + 1) * P)

            def chunk(k):
                pe.wait_ge(lo_done, MIX_CHUNK + k + 1)
                return (MIX_CHUNK + k) % 2

            def w_cols(slot, a, n):
                return w_hi[slot][:, a:a + n], w_lo[slot][:, a:a + n]

            def mixer():
                for cg, (_, n) in enumerate(LAT_COLS):
                    slot = chunk(LAT_AT + cg)
                    order = ([(t, k) for k in range(KD) for t in range(TOK)] if cg == 0
                             else [(t, k) for t in range(TOK) for k in range(KD)])
                    for t, k in order:
                        if cg == 0 and t == 0:
                            pe.wait_ge(h_ready[k % 2], KD // 2 + k // 2 + 1)
                        if cg == 2 and k == 0:
                            pe.wait_ge(lat_evac, t + 1)
                        last = product(bank[(4 * cg + t) % 8][:, 0:n], h_pair(k, toks(t)),
                                       w_cols(slot, k * n, n), k == 0, k == KD - 1)
                        if k == KD - 1:
                            last.then_inc(lat_ready, 1)
                for c in range(2):
                    slot = chunk(UPOOL_AT + c)
                    for g in range(2):
                        pe.wait_ge(lat_evac, TOK + 2 * c + g + 1)
                        for k in range(KD):
                            last = product(bank[4 + 2 * c + g][:, :], w_tile(slot, g * KD + k), h_pair(k),
                                           k == 0, k == KD - 1)
                        last.then_inc(u_ready, 1)
                pe.wait_ge(latn_ready, 1)
                pe.wait_ge(lat_evac, 3 * TOK)
                pe.wait_ge(u_evac, 1)
                for r in range(Q_TILES + KV_TILES):
                    ft = (r + Q_TILES) % (Q_TILES + KV_TILES)
                    for t in range(TOK):
                        last = nc.tensor.transpose(bank[r][:, toks(t)], lat[:, t, ft * P:(ft + 1) * P], ident[:, :])
                    last.then_inc(lat_t_ready, 1)
                slot = chunk(KV_AT)
                pe.wait_ge(u_evac, 4)
                pe.wait_ge(lat_lo_done, Q_TILES + KV_TILES)
                for kv in range(2):
                    for t in range(TOK):
                        for k in range(KV_TILES):
                            last = product(bank[(5 + 4 * kv + t) % 8][:, :],
                                           (lat_hi[:, Q_TILES + k, toks(t)], lat_lo[:, Q_TILES + k, toks(t)]),
                                           w_cols(slot, k * 1024 + kv * 512, 512), k == 0, k == KV_TILES - 1)
                        last.then_inc(kv_ready, 1)
                for c in range(2):
                    slot = chunk(Q_AT + c)
                    for t in range(TOK):
                        pe.wait_ge(kv_evac, 4 * c + t + 1)
                        for k in range(Q_TILES):
                            last = product(bank[(5 + 4 * c + t) % 8][:, 0:384],
                                           (lat_hi[:, k, toks(t)], lat_lo[:, k, toks(t)]),
                                           w_cols(slot, k * 384, 384), k == 0, k == Q_TILES - 1)
                        last.then_inc(q_ready, 1)
                for g in range(POOL_TILES):
                    pe.wait_ge(q_evac, g + 1)
                    pe.wait_ge(pooled_lo_done, g + 1)
                    last = product(bank[(5 + g) % 8][:, :], w_cols(slot, Q_TILES * 384 + g * P, P),
                                   (pooled_hi[:, g, :], pooled_lo[:, g, :]), True, True)
                    last.then_inc(group_ready, 1)
                for m in range(KD):
                    if m % 4 == 0:
                        slot = chunk(PP_AT + m // 4)
                    if m < 4:
                        pe.wait_ge(q_evac, 4 + m + 1)
                    for k in range(POOL_TILES):
                        if m == 0:
                            pe.wait_ge(group_lo_done, k + 1)
                        last = product(bank[(1 + m) % 8][:, :], w_tile(slot, m % 4 * 4 + k),
                                       (group_hi[:, k, :], group_lo[:, k, :]), k == 0, k == POOL_TILES - 1)
                    last.then_inc(proj_ready, 1)
                for h in range(HEADS):
                    for qk in range(2):
                        r = 2 * h + qk
                        if r < 8:
                            pe.wait_ge(proj_evac, r + 1)
                        else:
                            pe.wait_ge((q_t_evac, k_t_evac)[qk], h - 3)
                        pe.wait_ge(qk_tok_ready, 2)
                        for t in range(TOK):
                            last = nc.tensor.transpose(bank[(1 + r) % 8][0:HEAD, toks(t)], qk_tok[:, qk, t, h, :],
                                                       ident[:, :])
                        last.then_inc(qk_t_ready, 1)
                pe.wait_ge(q_t_evac, HEADS)
                pe.wait_ge(k_t_evac, HEADS)
                pe.wait_ge(mask_ready, 2)

                def head(i, s):
                    h = 2 * i + s
                    pe.wait_ge(q_now_ready, h + 1)
                    for qt in range(TOK):
                        nc.tensor.matmul(bank[qt][:, 0:(qt + 1) * P], q_now[0:HEAD, toks(qt)],
                                         k_t[0:HEAD, bass.ds(h, 1), 0:(qt + 1) * P], start=True, stop=False)
                        nc.tensor.matmul(bank[qt][:, toks(qt)], ident_r[:, :], mask_r[:, :],
                                         start=False, stop=True).then_inc(scores_ready, 1)
                    pe.wait_ge(lo_done, MIX_CHUNK + GATE_AT + h + 1)

                    def gate(g):
                        for k in range(KD):
                            last = product(bank[4 + g][:, :], w_tile(s, g * KD + k), h_pair(k), k == 0, k == KD - 1)
                        return last

                    gate(0).then_inc(gate_ready, 1)
                    pe.wait_ge(p_scaled, TOK * h + TOK)
                    for b, (qt, kt) in enumerate(P_BLOCKS):
                        last = nc.tensor.transpose(bank[b // 4][:, toks(b % 4)],
                                                   p_tok[:, qt * (qt + 1) // 2 + kt, :], ident[:, :])
                        if b % 4 == 3 or b == 9:
                            last.then_inc(p_t_ready, 1)
                    last = gate(1)
                    last.then_inc(gate_ready, 1)
                    pe.wait_ge(p_lo_done, 3 * h + 3)
                    pe.wait_ge(v_lo_done, h + 1)
                    pe.wait_ge(v_zero, 4)
                    v_cols = slice((1 - s) * V_DIM, (3 - s) * V_DIM)
                    if s == 0:
                        pe.wait_ge(attn_taken, i + 1)
                    for kt in range(TOK):
                        at = P_BLOCKS.index((kt, kt))
                        p_hi_kt, p_lo_kt = (p[:, at:at + TOK - kt, :].rearrange("p b q -> p (b q)") for p in (p_hi, p_lo))
                        last = product(bank[6][:, kt * P:S], (v_hi[:, kt, v_cols], v_lo[:, kt, v_cols]),
                                       (p_hi_kt, p_lo_kt), s + kt == 0, s * kt == TOK - 1)
                    last.then_inc(pv_ready, 1)

                with pe.Fori(0, HEADS // 2) as i:
                    for s in range(2):
                        head(i, s)
                for m in range(KD):
                    if m % 4 == 0:
                        slot = chunk(MLA_AT + m // 4)
                    if m < 2:
                        pe.wait_ge(tanh_done, 2 * HEADS - 1 + m)
                    for k in range(4):
                        if m == 0:
                            pe.wait_ge(attn_taken, k + 2)
                        last = product(bank[(4 + m) % 8][:, :], w_tile(slot, m % 4 * 4 + k),
                                       (attn_hi[:, k, :], attn_lo[:, k, :]), k == 0, k == 3)
                    last.then_inc(mla_ready, 1)
                pe.wait_ge(merged_ready, 2)
                for c in range(4):
                    slot = chunk(WOUT_AT + c)
                    for g in range(2):
                        m = 2 * c + g
                        if m >= 4:
                            pe.wait_ge(out_evac, KD + m - 1)
                        for k in range(KD):
                            if m == 0:
                                pe.wait_ge(merged_lo_done, k + 1)
                            last = product(bank[4 + m % 4][:, :], w_tile(slot, g * KD + k), h_pair(k),
                                           k == 0, k == KD - 1)
                    last.then_inc(pe_used, 1)

            pe.wait_ge(ones_ready, 1)
            pe.wait_ge(ones_r_ready, 1)
            reduce_first(0)
            reduce_first(1)
            norm(0)
            norm_wide(0)
            reduce_first(2)
            reduce_first(3)
            ffn(0)
            norm(1)
            norm_wide(1)
            mixer()
            norm(2)
            norm_wide(2)
            ffn(1)

        @block.scalar
        def _(act):
            def split(pair, slot, size, used=None):
                act.wait_ge(raw_in[slot], 16 * (pair + 1))
                if used:
                    act.wait_ge(*used)
                nc.scalar.activation(w_hi[slot][:, 0:size], w_raw[slot][:, 0:size], ACT.Copy).then_inc(hi_done, 1)

            def load_table(n, func):
                nc.scalar.activation(warm[:, n:n + 1], ident[:, 0:1], func)

            def square_x(m, count):
                act.wait_ge(sq_added, count)
                nc.scalar.activation(square, x[:, bass.ds(m, 1), :], ACT.Square).then_inc(sq_done, 1)

            def first_high(n):
                act.wait_ge(first_step[n], 8)
                if n >= 2:
                    act.wait_ge(ada_summed, n - 1)
                acc, hi, _ = sums_of[n % 2]
                nc.scalar.activation(hi[:, :], acc[:, :], ACT.Copy).then_inc(acc_hi_done, 1)

            def ada_high(group):
                act.wait_ge(ada_step, 8 * (group - ADA_START) + 8)
                act.wait_ge(ada_summed, group)
                nc.scalar.activation(acc_hi[:, :], ada_acc[:, :], ACT.Copy).then_inc(acc_hi_done, 1)

            def norm(l):
                act.wait_ge(var_ready, l + 1)
                nc.scalar.activation(std[:, :], var[:, :], ACT.Sqrt).then_inc(std_ready, 1)
                load_table(2 + l, (ACT.Silu, ACT.Sqrt, ACT.Silu)[l])

            def norm_high(l):
                shift = 3 * KD * l
                for m in range(KD):
                    act.wait_ge(scaled_ready, KD * l + m + 1)
                    nc.scalar.activation(h_hi[:, m, :], scaled[:, m % 2, :], ACT.Identity,
                                         scale=gain_mod[:, m:m + 1], bias=mod[:, shift + m:shift + m + 1])\
                        .then_inc(h_hi_ready, 1)

            def mix_split(k):
                used = chunk_used[k - 2] if k >= 2 else (pe_used, FFN_CHUNKS - 1 + k)
                split((MIX_CHUNK + k) // 2, k % 2, MIX_SIZES[k], used)

            def mixer():
                def copy(dst, src, done):
                    nc.scalar.activation(dst, src, ACT.Copy).then_inc(done, 1)

                def lat_out(r):
                    at, n = LAT_COLS[r // TOK]
                    act.wait_ge(lat_ready, r + 1)
                    copy(lat[:, r % TOK, at:at + n], bank[r % 8][:, 0:n], lat_evac)

                def u_out(g):
                    act.wait_ge(u_ready, g + 1)
                    copy(u_pad[:, g, 16:16 + S], bank[4 + g][:, :], u_evac)

                for c in range(3):
                    mix_split(c + 1)
                    for t in range(TOK):
                        lat_out(TOK * c + t)
                act.wait_ge(h_ready[0], KD)
                act.wait_ge(h_ready[1], KD)
                act.wait_ge(lat_evac, 3 * TOK)
                for r in range(2):
                    act.wait_ge(msq_used, r)
                    nc.scalar.activation(squares[:, :, 0:LAT], lat[:, 2 * r:2 * r + 2, :], ACT.Square)\
                        .then_inc(msq_done, 1)
                act.wait_ge(mvar_ready, 1)
                nc.scalar.activation(mstd[:, 0:3 * TOK], mvar[:, 0:3 * TOK], ACT.Sqrt).then_inc(mstd_ready, 1)
                mix_split(4)
                u_out(0)
                u_out(1)
                act.wait_ge(angle_ready, 1)
                nc.scalar.activation(sin[:, :, 0:16], angle[0][:, :, :], ACT.Sin, scale=-1.0).then_inc(trig_ready, 1)
                nc.scalar.activation(sin[:, :, 16:32], angle[0][:, :, :], ACT.Sin).then_inc(trig_ready, 1)
                nc.scalar.activation(cos[:, :, 0:16], angle[1][:, :, :], ACT.Sin).then_inc(trig_ready, 1)
                nc.scalar.activation(cos[:, :, 16:32], angle[1][:, :, :], ACT.Sin).then_inc(trig_ready, 1)
                mix_split(5)
                u_out(2)
                u_out(3)
                for r in range(Q_TILES + KV_TILES):
                    ft = (r + Q_TILES) % (Q_TILES + KV_TILES)
                    act.wait_ge(lat_t_ready, r + 1)
                    nc.scalar.activation(lat_hi[:, ft, :], bank[r][:, :], ACT.Copy, scale=mixc[:, LG_AT + ft:LG_AT + ft + 1])\
                        .then_inc(lat_hi_done, 1)
                mix_split(6)
                for r in range(8):
                    kv, t = r // 4, r % 4
                    act.wait_ge(kv_ready, r + 1)
                    src = bank[(5 + r) % 8][:, :]
                    if kv == 0:
                        copy(qk_tok[:, 1, t, :, 0:NOPE], src.rearrange("p (h d) -> p h d", h=HEADS), kv_evac)
                    else:
                        copy(v_tok[:, t, :], src, kv_evac)
                mix_split(7)

                def head_squares(qk, half, width):
                    act.wait_ge(msq_used, 4 - 2 * qk + half)
                    buf = squares[:, :, 0:HEADS * width].rearrange("p t (h d) -> p t h d", h=HEADS)
                    for t in range(2):
                        ins = nc.scalar.activation(buf[:, t], qk_tok[:, qk, 2 * half + t, :, 0:width], ACT.Square)
                    ins.then_inc(msq_done, 1)

                act.wait_ge(kv_evac, 8)
                head_squares(1, 0, NOPE)
                head_squares(1, 1, NOPE)
                act.wait_ge(mvar_ready, 2)
                nc.scalar.activation(mstd[:, 2 * HEADS * TOK:], mvar[:, 2 * HEADS * TOK:], ACT.Sqrt)\
                    .then_inc(mstd_ready, 1)

                def q_out(r):
                    c, t = r // 4, r % 4
                    act.wait_ge(q_ready, r + 1)
                    copy(qk_tok[:, 0, t, 4 * c:4 * c + 4, :],
                         bank[(5 + r) % 8][:, 0:384].rearrange("p (h d) -> p h d", h=4), q_evac)

                for r in range(4):
                    q_out(r)
                for g in range(POOL_TILES):
                    act.wait_ge(pooled_ready, g + 1)
                    copy(pooled_hi[:, g, :], u_pad[:, g, 16:16 + S], pooled_hi_done)
                for r in range(4, 8):
                    q_out(r)
                mix_split(8)
                for g in range(POOL_TILES):
                    act.wait_ge(group_ready, g + 1)
                    nc.scalar.activation(group_hi[:, g, :], bank[(5 + g) % 8][:, :], ACT.Copy,
                                         scale=mixc[:, PS_AT + g:PS_AT + g + 1]).then_inc(group_hi_done, 1)
                mix_split(9)
                act.wait_ge(q_evac, 8)
                head_squares(0, 0, HEAD)
                head_squares(0, 1, HEAD)
                act.wait_ge(mvar_ready, 3)
                nc.scalar.activation(mstd[:, 0:2 * HEADS * TOK], mvar[:, 0:2 * HEADS * TOK], ACT.Sqrt)\
                    .then_inc(mstd_ready, 1)
                load_table(6, ACT.Exp)
                for m in range(KD):
                    if m == 4:
                        mix_split(10)
                    act.wait_ge(proj_ready, m + 1)
                    copy(br_pool[:, m, :], bank[(1 + m) % 8][:, :], proj_evac)
                for h in range(HEADS):
                    act.wait_ge(qk_t_ready, 2 * h + 1)
                    copy(q_t[0:HEAD, h, :], bank[(1 + 2 * h) % 8][0:HEAD, :], q_t_evac)
                act.wait_ge(q_t_evac, HEADS)
                act.wait_ge(qk_t_ready, 2 * HEADS)
                copy(mask_r[:, :], mixc[:, MASK_AT:MASK_AT + P], mask_ready)
                copy(ident_r[:, :], ident[:, :], mask_ready)

                def head(i, s, half):
                    h = HEADS // 2 * half + 2 * i + s
                    copy(q_now[0:HEAD, :], q_t[0:HEAD, bass.ds(h, 1), :].rearrange("p a s -> p (a s)"), q_now_ready)
                    for qt in range(TOK):
                        at = qt * (qt + 1) // 2
                        act.wait_ge(max_ready, TOK * h + qt + 1)
                        nc.scalar.activation(p_tok[:, at:at + qt + 1, :].rearrange("p b q -> p (b q)"),
                                             bank[qt][:, 0:(qt + 1) * P], ACT.Exp, bias=row_max[:, qt:qt + 1],
                                             accum_out=row_sum[:, qt:qt + 1]).then_inc(p_ready, 1)

                    def gate(g):
                        act.wait_ge(gate_ready, 2 * h + g + 1)
                        if half:
                            dst = tanh_mla[:, bass.ds(2 * (2 * i + s) + g, 1), :].rearrange("p a s -> p (a s)")
                        else:
                            dst = scaled[:, g, :]
                        nc.scalar.activation(dst, bank[4 + g][:, :], ACT.Tanh, scale=0.5).then_inc(tanh_done, 1)

                    gate(0)
                    split((MIX_CHUNK + GATE_AT) // 2 + HEADS // 4 * half + i + (s + 1) // 2, 1 - s, SLOT)
                    copy(v_hi[:, :, V_DIM:2 * V_DIM], v_tok[:, :, bass.ds(V_DIM * h, V_DIM)], v_hi_done)
                    for b, (at, n) in enumerate(P_PARTS):
                        act.wait_ge(p_t_ready, 3 * h + b + 1)
                        copy(p_hi[:, at:at + n, :].rearrange("p b q -> p (b q)"), bank[b][:, 0:n * P], p_hi_done)
                    gate(1)

                for half in range(2):
                    with act.Fori(0, HEADS // 4) as i:
                        for s in range(2):
                            head(i, s, half)
                for m in range(KD):
                    if m % 4 == 0:
                        mix_split(19 + m // 4)
                    act.wait_ge(merged_ready, m + 1)
                    copy(h_hi[:, m, :], h32[:, m % 2, :], merged_hi_done)
                load_table(7, ACT.Sqrt)
                for c in range(4):
                    if c < 3:
                        mix_split(21 + c)
                    else:
                        split(FIRST_CHUNK[1] // 2, 0, IN_ELEMS, (pe_used, FFN_USED[1] - 1))
                    for g in range(2):
                        m = 2 * c + g
                        act.wait_ge(out_evac, KD + m + 3)
                        square_x(m, KD + m)

            def ffn(f, after):
                n0, u0 = FIRST_CHUNK[f], FFN_USED[f]

                def up(i, first, last):
                    for s in range(2):
                        j = 2 * i + s
                        split((n0 + s + 1) // 2 + i, 1 - s, OUT_ELEMS if last and s else IN_ELEMS,
                              (pe_used, u0 + j) if not (first and f == 0 and s == 0) else None)
                        act.wait_ge(pe_used, u0 + j + 1)
                        act.wait_ge(gu_evac, NF * f + j + 2)
                        nc.scalar.activation(silu_g, bank[2 * s][:, :], ACT.Silu).then_inc(silu_done, 1)
                        act.wait_ge(gu_evac, NF * f + j + 3)
                        nc.scalar.activation(act_hi[f][:, bass.ds(j, 1), :], prod, ACT.Copy).then_inc(act_hi_done, 1)
                        if f == 0 and s:
                            ada_high(ADA_START + i)

                up(0, True, False)
                with act.Fori(1, NFH - 1) as i:
                    up(i, False, False)
                up(NFH - 1, False, True)

                if f == 0:
                    load_table(0, ACT.Sqrt)

                def down(i, last):
                    for s in range(4):
                        q = NF + 4 * i + s
                        if not (last and s == 3):
                            split((n0 + NF + s + 1) // 2 + 2 * i, (s + 1) % 2, OUT_ELEMS, (pe_used, u0 + q))
                        elif after:
                            after()
                        if s % 2:
                            m = 2 * i + s // 2
                            act.wait_ge(out_evac, KD * 2 * f + m + 3)
                            if f == 0:
                                square_x(m, m)
                        if f == 0 and s == 3 and not last:
                            ada_high(ADA_START + NFH + i)

                with act.Fori(0, 3) as i:
                    down(i, False)
                down(3, True)

            act.wait_ge(c_in, 16)
            nc.scalar.activation(c_act[:, :], c_raw[:, :], ACT.Silu).then_inc(c_ready, 1)
            act.wait_ge(x_in, 16)
            nc.scalar.activation(sq_first[:, :, :], x[:, :, :], ACT.Square).then_inc(sq_done, 1)
            act.wait_ge(const_in, 48)
            load_table(1, ACT.Sqrt)
            first_high(0)
            first_high(1)
            norm(0)
            split(0, 0, IN_ELEMS)
            first_high(2)
            first_high(3)
            norm_high(0)
            for odd in range(2):
                act.wait_ge(h_ready[odd], KD // 2)
            ffn(0, lambda: mix_split(0))
            norm(1)
            norm_high(1)
            mixer()
            norm(2)
            norm_high(2)
            ffn(1, None)

        @block.vector
        def _(dve):
            links = [0]

            def link(ins):
                links[0] += 1
                ins.then_inc(small, 1)
                dve.wait_ge(small, links[0])

            def split(n, slot, size):
                dve.wait_ge(hi_done, n + 1)
                nc.vector.tensor_tensor(w_lo[slot][:, 0:size], w_raw[slot][:, 0:size],
                                        w_hi[slot][:, 0:size].bitcast(F32), ALU.subtract).then_inc(lo_done, 1)

            def add_first(pair, kts):
                for kt in kts:
                    for b in range(2):
                        n = 2 * pair + b
                        if kt % 4 == 0:
                            dve.wait_ge(ada_first_in[2 * n + kt // 4], 16)
                        if kt == 0 and pair:
                            dve.wait_ge(acc_lo_done, n - 1)
                        if kt:
                            dve.wait_ge(first_step[n], kt)
                        add_to(sums_of[b][0], ada_first[:, FIRST_GROUPS[n], kt, :], kt, first_step[n])

            def add_ada(group, kts):
                for kt in kts:
                    dve.wait_ge(ada_in[kt % 4], 16 * (2 * (group - ADA_START) + kt // 4 + 1))
                    if kt:
                        dve.wait_ge(ada_step, 8 * (group - ADA_START) + kt)
                    else:
                        dve.wait_ge(acc_lo_done, group)
                    add_to(ada_acc, ada_raw[:, kt % 4, :], kt, ada_step)

            def add_to(acc, raw, kt, done):
                if kt == 0:
                    nc.vector.tensor_scalar(acc[:, :], raw, c_act[:, 0:1], None, ALU.mult).then_inc(done, 1)
                else:
                    nc.vector.scalar_tensor_tensor(out=acc[:, :], in0=raw, scalar=c_act[:, kt:kt + 1],
                                                   in1=acc[:, :], op0=ALU.mult, op1=ALU.add).then_inc(done, 1)

            def ada_low(count, buf=0):
                acc, hi, lo = sums_of[buf]
                dve.wait_ge(acc_hi_done, count)
                nc.vector.tensor_tensor(lo[:, :], acc[:, :], hi[:, :].bitcast(F32), ALU.subtract)\
                    .then_inc(acc_lo_done, 1)

            def keep_first(pair):
                dve.wait_ge(ada_summed, 2 * pair + 2)
                for b in range(2):
                    add_bias(FIRST_GROUPS[2 * pair + b])

            def keep_mod(group):
                dve.wait_ge(ada_summed, group + 1)
                add_bias(group)

            def add_bias(group):
                cols = bass.ds(4 * group, 4)
                sums = ADA_BANK[:, bass.ds(8 * group, 8)].rearrange("p (c two) -> p c two", two=2)[:, :, 0]
                nc.vector.tensor_tensor(mod[:, cols], sums, bias_ada[:, cols], ALU.add).then_inc(mod_ready, 1)

            def sum_squares(l):
                dve.wait_ge(sq_done, KD * l + 1)
                dve.wait_ge(sq_added, KD * l - 1)
                nc.vector.tensor_tensor(ssq[:, :], ssq[:, :], square, ALU.add).then_inc(ssq_ready, 1)

            def norm_start(l):
                dve.wait_ge(stat_ready, l + 1)
                nc.vector.tensor_scalar(var[:, :], STAT_BANK[:, 0:4], 1.0 / D, EPS, ALU.mult, ALU.add)\
                    .then_inc(var_ready, 1)

            def norm(l):
                dve.wait_ge(std_ready, l + 1)
                link(nc.vector.reciprocal(rstd[:, :], std[:, :]))
                link(nc.vector.tensor_tensor(newton[:, :], rstd[:, :], rstd[:, :], ALU.mult))
                link(nc.vector.scalar_tensor_tensor(out=newton[:, :], in0=newton[:, :], scalar=-0.5, in1=var[:, :],
                                                    op0=ALU.mult, op1=ALU.mult))
                link(nc.vector.scalar_tensor_tensor(out=rstd[:, :], in0=newton[:, :], scalar=1.5, in1=rstd[:, :],
                                                    op0=ALU.add, op1=ALU.mult))
                nc.vector.tensor_tensor(diag.rearrange("p (t q) -> p t q", t=4),
                                        ident[:, :].unsqueeze(1).broadcast_to([P, 4, P]),
                                        rstd[:, :].unsqueeze(2).broadcast_to([P, 4, P]), ALU.mult)\
                    .then_inc(diag_ready, 1)

            def modulation(l):
                scale, gate = mod[:, 3 * KD * l + KD:3 * KD * l + 2 * KD], mod[:, 3 * KD * l + 2 * KD:3 * KD * (l + 1)]
                return scale, gate

            def modulated(l):
                scale, _ = modulation(l)
                link(nc.vector.scalar_tensor_tensor(out=gain_mod[:, :], in0=scale, scalar=1.0,
                                                    in1=gain[:, KD * l:KD * (l + 1)], op0=ALU.add, op1=ALU.mult))
                dve.wait_ge(rstd_wide, l + 1)
                shift = 3 * KD * l
                for m in range(KD + 1):
                    if m < KD:
                        if m >= 2:
                            dve.wait_ge(h_hi_ready, KD * l + m - 1)
                            dve.wait_ge(h32_ready, KD * l + m - 1)
                        nc.vector.tensor_tensor(scaled[:, m % 2, :], x[:, m, :], bank[4][:, :], ALU.mult)\
                            .then_inc(scaled_ready, 1)
                    if m:
                        n = m - 1
                        dve.wait_ge(scaled_ready, KD * l + n + 1)
                        if n >= 2:
                            dve.wait_ge(h_ready[n % 2], KD // 2 * l + n // 2)
                        nc.vector.tensor_scalar(h32[:, n % 2, :], scaled[:, n % 2, :], gain_mod[:, n:n + 1],
                                                mod[:, shift + n:shift + n + 1], ALU.mult, ALU.add)\
                            .then_inc(h32_ready, 1)
                        if n % 2 == 0:
                            dve.wait_ge(h32_ready, KD * l + n + 1)
                            dve.wait_ge(h_hi_ready, KD * l + n + 1)
                            nc.vector.tensor_tensor(h_lo[:, n, :], h32[:, n % 2, :], h_hi[:, n, :].bitcast(F32),
                                                    ALU.subtract).then_inc(h_ready[0], 1)

            def mix_split(k):
                split(MIX_CHUNK + k, k % 2, MIX_SIZES[k])

            def mixer():
                def tt(dst, a, b, op):
                    return nc.vector.tensor_tensor(dst, a, b, op)

                def ts(dst, a, s1, s2, op0, op1):
                    return nc.vector.tensor_scalar(dst, a, s1, s2, op0, op1)

                def wide(v, n):
                    return v.unsqueeze(len(v.shape)).broadcast_to([*v.shape, n])

                def rsqrt(at, n):
                    r, w, v = (z[:, at:at + n] for z in (mrstd, mnewton, mvar))
                    link(nc.vector.reciprocal(r, mstd[:, at:at + n]))
                    link(tt(w, r, r, ALU.mult))
                    link(nc.vector.scalar_tensor_tensor(out=w, in0=w, scalar=-0.5, in1=v, op0=ALU.mult, op1=ALU.mult))
                    return nc.vector.scalar_tensor_tensor(out=r, in0=w, scalar=1.5, in1=r, op0=ALU.add, op1=ALU.mult)

                mix_split(1)
                dve.wait_ge(mixc_in, 32)
                dve.wait_ge(h_ready[0], KD)
                dve.wait_ge(h_ready[1], KD)
                pos, ang, turns = mnewton[:, 0:TOK], angle[2][:, :, :], angle[3][:, :, :]
                link(nc.vector.tensor_copy(pos, pos_int[:, :]))
                link(tt(ang, wide(pos, 16), mixc[:, FREQ_AT:FREQ_AT + 16].unsqueeze(1).broadcast_to([P, TOK, 16]),
                        ALU.mult))
                for fn in range(2):
                    red = angle[fn][:, :, :]
                    link(ts(turns, ang, 1.0 / (2.0 * 3.141592653589793), 0.25 * fn, ALU.mult, ALU.add))
                    link(ts(turns, turns, MAGIC, MAGIC, ALU.add, ALU.subtract))
                    src = ang
                    for part in TWO_PI:
                        link(nc.vector.scalar_tensor_tensor(out=red, in0=turns, scalar=-part, in1=src,
                                                            op0=ALU.mult, op1=ALU.add))
                        src = red
                    if fn:
                        link(ts(red, red, 1.5707963267948966, 3.1415925, ALU.add, ALU.min))
                        nc.vector.tensor_scalar(red, red, -3.1415925, None, ALU.max).then_inc(angle_ready, 1)
                    else:
                        link(ts(red, red, -3.1415925, 3.1415925, ALU.max, ALU.min))
                nc.vector.tensor_scalar(mixc[:, QG_AT:QG_AT + HEAD], mixc[:, QG_AT:QG_AT + HEAD], ATTN_SCALE, None,
                                        ALU.mult).then_inc(mixc_scaled, 1)
                mix_split(2)
                mix_split(3)
                lat_parts = ((0, Q_RANK), (Q_RANK, KV_RANK), (Q_RANK + KV_RANK, ROPE))
                for r in range(2):
                    dve.wait_ge(msq_done, r + 1)
                    for j, (at, n) in enumerate(lat_parts):
                        last = nc.vector.tensor_reduce(mvar[:, TOK * j + 2 * r:TOK * j + 2 * r + 2],
                                                       squares[:, :, at:at + n], AX_X, ALU.add)
                    last.then_inc(msq_used, 1)
                dve.wait_ge(msq_used, 2)
                for j, (at, n) in enumerate(lat_parts):
                    last = ts(mvar[:, TOK * j:TOK * j + TOK], mvar[:, TOK * j:TOK * j + TOK], 1.0 / n, EPS,
                              ALU.mult, ALU.add)
                last.then_inc(mvar_ready, 1)
                dve.wait_ge(mvar_ready, 1)
                dve.wait_ge(mstd_ready, 1)
                link(rsqrt(0, 3 * TOK))
                for j, (at, n) in enumerate(lat_parts):
                    last = tt(lat[:, :, at:at + n], lat[:, :, at:at + n], wide(mrstd[:, TOK * j:TOK * j + TOK], n),
                              ALU.mult)
                last.then_inc(latn_ready, 1)
                mix_split(4)

                def pooled_low(g):
                    dve.wait_ge(pooled_hi_done, g + 1)
                    tt(pooled_lo[:, g, :], u_pad[:, g, 16:16 + S], pooled_hi[:, g, :].bitcast(F32),
                       ALU.subtract).then_inc(pooled_lo_done, 1)

                mix_split(5)
                for r in range(Q_TILES + KV_TILES):
                    ft = (r + Q_TILES) % (Q_TILES + KV_TILES)
                    dve.wait_ge(lat_hi_done, r + 1)
                    nc.vector.scalar_tensor_tensor(out=lat_lo[:, ft, :], in0=bank[r][:, :],
                                                   scalar=mixc[:, LG_AT + ft:LG_AT + ft + 1],
                                                   in1=lat_hi[:, ft, :].bitcast(F32), op0=ALU.mult,
                                                   op1=ALU.subtract).then_inc(lat_lo_done, 1)
                mix_split(6)

                def rotate(src, scratch):
                    a, b = scratch
                    c, s = cos[:, :, :], sin[:, :, :]
                    tt(a, src, c, ALU.mult)
                    lo, hi = slice(0, 16), slice(16, 32)
                    tt(b[..., lo], src[..., hi], s[..., lo], ALU.mult)
                    link(tt(b[..., hi], src[..., lo], s[..., hi], ALU.mult))
                    return a, b

                dve.wait_ge(trig_ready, 4)
                dve.wait_ge(latn_ready, 1)
                k_rope = lat[:, :, Q_RANK + KV_RANK:LAT]
                link(tt(k_rope, k_rope, mixc[:, KG_AT + NOPE:KG_AT + HEAD].unsqueeze(1).broadcast_to([P, TOK, ROPE]),
                        ALU.mult))
                a, b = rotate(k_rope, (krot[:, 0], krot[:, 1]))
                for t in range(TOK):
                    tt(qk_tok[:, 1, t, :, NOPE:HEAD], a[:, t, :].unsqueeze(1).broadcast_to([P, HEADS, ROPE]),
                       b[:, t, :].unsqueeze(1).broadcast_to([P, HEADS, ROPE]), ALU.add).then_inc(k_rope_done, 1)
                def head_sums(qk, half, width):
                    n = 2 + 2 * (1 - qk) + half + 1
                    dve.wait_ge(msq_done, n)
                    buf = squares[:, :, 0:HEADS * width].rearrange("p t (h d) -> p t h d", h=HEADS)
                    at = 2 * qk * TOK * HEADS + 2 * half * HEADS
                    last = nc.vector.tensor_reduce(mvar[:, at:at + 2 * HEADS].rearrange("p (t h) -> p t h", t=2),
                                                   buf[:, :, :, 0:NOPE], AX_X, ALU.add)
                    if qk == 0:
                        at += TOK * HEADS
                        last = nc.vector.tensor_reduce(mvar[:, at:at + 2 * HEADS].rearrange("p (t h) -> p t h", t=2),
                                                       buf[:, :, :, NOPE:HEAD], AX_X, ALU.add)
                    last.then_inc(msq_used, 1)

                mix_split(7)
                head_sums(1, 0, NOPE)
                head_sums(1, 1, NOPE)
                n = TOK * HEADS
                dve.wait_ge(msq_used, 4)
                ts(mvar[:, 2 * n:3 * n], mvar[:, 2 * n:3 * n], 1.0 / NOPE, EPS, ALU.mult, ALU.add)\
                    .then_inc(mvar_ready, 1)
                dve.wait_ge(mvar_ready, 2)
                dve.wait_ge(mstd_ready, 2)
                rsqrt(2 * n, n).then_inc(k_stat_ready, 1)
                for g in range(POOL_TILES):
                    pooled_low(g)
                mix_split(8)

                for g in range(POOL_TILES):
                    dve.wait_ge(group_hi_done, g + 1)
                    nc.vector.scalar_tensor_tensor(out=group_lo[:, g, :], in0=bank[(5 + g) % 8][:, :],
                                                   scalar=mixc[:, PS_AT + g:PS_AT + g + 1],
                                                   in1=group_hi[:, g, :].bitcast(F32), op0=ALU.mult,
                                                   op1=ALU.subtract).then_inc(group_lo_done, 1)
                mix_split(9)
                head_sums(0, 0, HEAD)
                head_sums(0, 1, HEAD)
                dve.wait_ge(msq_used, 6)
                ts(mvar[:, 0:n], mvar[:, 0:n], 1.0 / NOPE, EPS, ALU.mult, ALU.add)
                ts(mvar[:, n:2 * n], mvar[:, n:2 * n], 1.0 / ROPE, EPS, ALU.mult, ALU.add)\
                    .then_inc(mvar_ready, 1)
                dve.wait_ge(mvar_ready, 3)
                dve.wait_ge(mstd_ready, 3)
                link(rsqrt(0, 2 * n))

                def heads_of(qk):
                    return qk_tok[:, qk].rearrange("p t h d -> p (t h) d")

                dve.wait_ge(mixc_scaled, 1)
                q = heads_of(0)
                tt(q[:, :, 0:NOPE], q[:, :, 0:NOPE], wide(mrstd[:, 0:n], NOPE), ALU.mult)
                link(tt(q[:, :, NOPE:HEAD], q[:, :, NOPE:HEAD], wide(mrstd[:, n:2 * n], ROPE), ALU.mult))
                mix_split(10)

                def gains_of(at, width):
                    return mixc[:, at:at + width].unsqueeze(1).broadcast_to([P, n, width])

                link(tt(q, q, gains_of(QG_AT, HEAD), ALU.mult))
                for half in range(2):
                    for t in range(2):
                        tok = 2 * half + t
                        src = qk_tok[:, 0, tok, :, NOPE:HEAD]
                        a, b = rot_a[:, tok], rot_b[:, tok]
                        c, s = (v[:, tok, :].unsqueeze(1).broadcast_to([P, HEADS, ROPE]) for v in (cos, sin))
                        tt(a, src, c, ALU.mult)
                        tt(b[:, :, 0:16], src[:, :, 16:32], s[:, :, 0:16], ALU.mult)
                        link(tt(b[:, :, 16:32], src[:, :, 0:16], s[:, :, 16:32], ALU.mult))
                last = tt(q[:, :, NOPE:HEAD], rot_a[:, :, :, :].rearrange("p t h d -> p (t h) d"),
                          rot_b[:, :, :, :].rearrange("p t h d -> p (t h) d"), ALU.add)
                last.then_inc(qk_tok_ready, 1)
                for h in range(HEADS):
                    dve.wait_ge(qk_t_ready, 2 * h + 2)
                    nc.vector.tensor_copy(k_t[0:HEAD, h, :], bank[(2 + 2 * h) % 8][0:HEAD, :]).then_inc(k_t_evac, 1)

                dve.wait_ge(k_t_evac, HEADS)
                nc.vector.memset(row_inv[:, :], 0.0).then_inc(attn_taken, 1)

                def head(i, s, half):
                    h = HEADS // 2 * half + 2 * i + s
                    for qt in range(TOK):
                        dve.wait_ge(scores_ready, TOK * h + qt + 1)
                        nc.vector.tensor_reduce(row_max[:, qt:qt + 1], bank[qt][:, 0:(qt + 1) * P], AX_X, ALU.max,
                                                negate=True).then_inc(max_ready, 1)

                    def gate(g):
                        if not half:
                            dve.wait_ge(tanh_done, 2 * h + g + 1)
                            part = br_pool[:, bass.ds(2 * (2 * i + s) + g, 1), :].rearrange("p a s -> p (a s)")
                            nc.vector.scalar_tensor_tensor(out=part, in0=scaled[:, g, :], scalar=1.0, in1=part,
                                                           op0=ALU.add, op1=ALU.mult).then_inc(gated, 1)

                    dve.wait_ge(p_ready, TOK * h + TOK)
                    nc.vector.reciprocal(row_inv[:, :], row_sum[:, :]).then_inc(inv_done, 1)
                    dve.wait_ge(inv_done, h + 1)
                    for qt in range(TOK):
                        at = qt * (qt + 1) // 2
                        p_rows = p_tok[:, at:at + qt + 1, :]
                        nc.vector.tensor_scalar(p_rows, p_rows, row_inv[:, qt:qt + 1], None, ALU.mult)\
                            .then_inc(p_scaled, 1)
                    split(MIX_CHUNK + GATE_AT + h + 1, 1 - s, SLOT)
                    dve.wait_ge(v_hi_done, h + 1)
                    nc.vector.tensor_tensor(v_lo[:, :, V_DIM:2 * V_DIM], v_tok[:, :, bass.ds(V_DIM * h, V_DIM)],
                                            v_hi[:, :, V_DIM:2 * V_DIM].bitcast(F32), ALU.subtract).then_inc(v_lo_done, 1)
                    for b, (at, n) in enumerate(P_PARTS):
                        dve.wait_ge(p_hi_done, 3 * h + b + 1)
                        nc.vector.tensor_tensor(p_lo[:, at:at + n, :].rearrange("p b q -> p (b q)"),
                                                bank[b][:, 0:n * P],
                                                p_hi[:, at:at + n, :].bitcast(F32).rearrange("p b q -> p (b q)"),
                                                ALU.subtract).then_inc(p_lo_done, 1)
                    gate(0)
                    gate(1)
                    if s:
                        dve.wait_ge(pv_ready, h + 1)
                        tile = bass.ds(HEADS // 4 * half + i, 1)
                        src, hi = bank[6][:, :].unsqueeze(1), attn_hi[:, tile, :]
                        nc.vector.tensor_copy(hi, src).then_inc(attn_hi_done, 1)
                        dve.wait_ge(attn_hi_done, HEADS // 4 * half + i + 1)
                        nc.vector.tensor_tensor(attn_lo[:, tile, :], src, hi.bitcast(F32), ALU.subtract)\
                            .then_inc(attn_taken, 1)

                for half in range(2):
                    with dve.Fori(0, HEADS // 4) as i:
                        for s in range(2):
                            head(i, s, half)
                _, gate_cols = modulation(1)
                link(nc.vector.tensor_scalar(out_gate[:, :], gate_cols, 0.5, None, ALU.mult))
                def merged_low(m):
                    dve.wait_ge(merged_hi_done, m + 1)
                    tt(h_lo[:, m, :], h32[:, m % 2, :], h_hi[:, m, :].bitcast(F32), ALU.subtract)\
                        .then_inc(merged_lo_done, 1)

                for m in range(KD):
                    if m % 4 == 0:
                        mix_split(19 + m // 4)
                    dve.wait_ge(mla_ready, m + 1)
                    dve.wait_ge(tanh_done, 2 * HEADS)
                    nc.vector.scalar_tensor_tensor(out=tanh_mla[:, m, :], in0=tanh_mla[:, m, :], scalar=1.0,
                                                   in1=bank[(4 + m) % 8][:, :], op0=ALU.add, op1=ALU.mult)\
                        .then_inc(mla_gated, 1)
                    if m:
                        merged_low(m - 1)
                merged_low(KD - 1)
                for c in range(4):
                    if c < 3:
                        mix_split(21 + c)
                    else:
                        split(FIRST_CHUNK[1], 0, IN_ELEMS)
                    for g in range(2):
                        m = 2 * c + g
                        dve.wait_ge(pe_used, FFN_CHUNKS + c + 1)
                        nc.vector.scalar_tensor_tensor(out=x[:, m, :], in0=bank[4 + m % 4][:, :],
                                                       scalar=out_gate[:, m:m + 1], in1=x[:, m, :],
                                                       op0=ALU.mult, op1=ALU.add).then_inc(out_evac, 1)

            def ffn(f, after):
                n0, u0 = FIRST_CHUNK[f], FFN_USED[f]

                def up(i, first, last):
                    for s in range(2):
                        j = 2 * i + s
                        split(n0 + j + 1, 1 - s, OUT_ELEMS if last and s else IN_ELEMS)
                        if f == 0:
                            add_ada(ADA_START + i, range(4 * s, 4 * s + 4))
                        if not (f == 0 and first and s == 0):
                            dve.wait_ge(act_done, NF * f + j)
                        dve.wait_ge(silu_done, NF * f + j + 1)
                        nc.vector.tensor_tensor(prod, silu_g, bank[2 * s + 1][:, :], ALU.mult).then_inc(gu_evac, 1)
                        dve.wait_ge(act_hi_done, NF * f + j + 1)
                        nc.vector.tensor_tensor(act_lo[f][:, bass.ds(j, 1), :], prod.unsqueeze(1),
                                                act_hi[f][:, bass.ds(j, 1), :].bitcast(F32), ALU.subtract)\
                            .then_inc(act_done, 1)
                        if f == 0 and s == 0 and not first:
                            keep_mod(ADA_START + i - 1)
                        if f == 0 and s:
                            ada_low(ADA_START + i + 1)

                up(0, True, False)
                with dve.Fori(1, NFH - 1) as i:
                    up(i, False, False)
                up(NFH - 1, False, True)
                _, gate = modulation(2 * f)
                link(nc.vector.tensor_scalar(out_gate[:, :], gate, 0.5, None, ALU.mult))

                def down(i, last):
                    for s in range(4):
                        q = NF + 4 * i + s
                        if not (last and s == 3):
                            split(n0 + q + 1, (s + 1) % 2, OUT_ELEMS)
                        elif after:
                            after()
                        if f == 0 and s == 0:
                            keep_mod(ADA_START + NFH + i - 1)
                        if f == 0 and not last and s % 2 == 0:
                            add_ada(ADA_START + NFH + i, range(2 * s, 2 * s + 4))
                        if s % 2:
                            m = 2 * i + s // 2
                            dve.wait_ge(pe_used, u0 + q + 1)
                            xm = x[:, bass.ds(m, 1), :]
                            nc.vector.scalar_tensor_tensor(out=xm, in0=bank[4 + s // 2][:, :].unsqueeze(1),
                                                           scalar=out_gate[:, bass.ds(m, 1)], in1=xm,
                                                           op0=ALU.mult, op1=ALU.add).then_inc(out_evac, 1)
                        if f == 0 and s == 3 and not last:
                            ada_low(ADA_START + NFH + i + 1)

                with dve.Fori(0, 3) as i:
                    down(i, False)
                down(3, True)

            nc.vector.memset(ones[:, :], 1.0).then_inc(ones_ready, 1)
            nc.vector.memset(rstd[:, :], 0.0).then_inc(gu_evac, 2)
            nc.vector.memset(newton[:, :], 0.0).then_inc(out_evac, 2)
            dve.wait_ge(ones_ready, 1)
            nc.vector.tensor_copy(ones_r[:, :], ones[:, 0:2]).then_inc(ones_r_ready, 1)
            dve.wait_ge(c_ready, 1)
            add_first(0, range(8))
            ada_low(1, 0)
            ada_low(2, 1)
            add_first(1, range(4))
            dve.wait_ge(const_in, 48)
            keep_first(0)
            norm_start(0)
            split(0, 0, IN_ELEMS)
            norm(0)
            add_first(1, range(4, 8))
            ada_low(3, 0)
            ada_low(4, 1)
            keep_first(1)
            dve.wait_ge(mod_ready, ADA_START)
            modulated(0)
            ffn(0, lambda: mix_split(0))
            sum_squares(1)
            norm_start(1)
            norm(1)
            modulated(1)
            mixer()
            sum_squares(2)
            norm_start(2)
            norm(2)
            modulated(2)
            ffn(1, None)

        @block.gpsimd
        def _(pool):
            def squares_up(l):
                before = KD * (l - 1)
                pool.wait_ge(sq_done, before + 2)
                nc.gpsimd.tensor_copy(ssq[:, :], square).then_inc(sq_added, 1)
                with pool.Fori(1, KD - 1) as m:
                    pool.wait_ge(sq_done, m + (before + 2))
                    pool.wait_ge(sq_added, m + before)
                    nc.gpsimd.tensor_tensor(ssq[:, :], ssq[:, :], square, ALU.add).then_inc(sq_added, 1)
                if l == 1:
                    pool.wait_ge(ssq_ready, l + 1)
                    nc.gpsimd.memset(pool_note[:, :], 0.0).then_inc(sq_added, 1)

            def norm(l):
                for m in range(1, KD, 2):
                    pool.wait_ge(h32_ready, KD * l + m + 1)
                    pool.wait_ge(h_hi_ready, KD * l + m + 1)
                    nc.gpsimd.tensor_tensor(h_lo[:, m, :], h32[:, m % 2, :], h_hi[:, m, :].bitcast(F32),
                                            ALU.subtract).then_inc(h_ready[1], 1)

            chain = [0]

            def link(ins):
                chain[0] += 1
                ins.then_inc(pool_chain, 1)
                pool.wait_ge(pool_chain, chain[0])

            pool.wait_ge(sq_done, 1)
            link(nc.gpsimd.tensor_tensor(ssq[:, :], sq_first[:, 0, :], sq_first[:, 1, :], ALU.add))
            for m in range(2, KD - 1):
                link(nc.gpsimd.tensor_tensor(ssq[:, :], ssq[:, :], sq_first[:, m, :], ALU.add))
            nc.gpsimd.tensor_tensor(ssq[:, :], ssq[:, :], sq_first[:, KD - 1, :], ALU.add).then_inc(ssq_ready, 1)
            norm(0)
            squares_up(1)
            norm(1)

            pool.wait_ge(stat_ready, 2)
            link(nc.gpsimd.memset(u_pad[:, :, 0:16], 0.0))
            for n in range(2):
                link(nc.gpsimd.memset(window[n][:, 0:16], 0.0))
            pool.wait_ge(mixc_in, 32)
            for g in range(POOL_TILES):
                pool.wait_ge(u_evac, g + 1)
                if g:
                    pool.wait_ge(pooled_ready, g)
                src, real = u_pad[:, g, :], slice(16, 16 + S)
                for level in range(g + 1):
                    w, dst = 1 << level, window[level % 2]
                    link(nc.gpsimd.tensor_tensor(dst[:, real], src[:, real], src[:, 16 - w:16 + S - w], ALU.add))
                    src = dst
                link(nc.gpsimd.tensor_tensor(src[:, 16:32], src[:, 16:32],
                                             mixc[:, CORR_AT + 16 * g:CORR_AT + 16 * g + 16], ALU.mult))
                link(nc.gpsimd.tensor_scalar(src[:, real], src[:, real], 1.0 / (2 << g), None, ALU.mult))
                nc.gpsimd.tensor_tensor(u_pad[:, g, real], src[:, real], u_pad[:, g, real], ALU.subtract)\
                    .then_inc(pooled_ready, 1)
            pool.wait_ge(k_stat_ready, 1)
            n = TOK * HEADS
            k = qk_tok[:, 1].rearrange("p t h d -> p (t h) d")[:, :, 0:NOPE]
            link(nc.gpsimd.tensor_tensor(k, k, mrstd[:, 2 * n:3 * n].unsqueeze(2).broadcast_to([P, n, NOPE]), ALU.mult))
            nc.gpsimd.tensor_tensor(k, k, mixc[:, KG_AT:KG_AT + NOPE].unsqueeze(1).broadcast_to([P, n, NOPE]),
                                    ALU.mult).then_inc(qk_tok_ready, 1)
            pool.wait_ge(qk_t_ready, 2 * HEADS)
            for part in (v_hi, v_lo):
                for at in (0, 2 * V_DIM):
                    nc.gpsimd.tensor_scalar(part[:, :, at:at + V_DIM],
                                            ident[:, 0:V_DIM].unsqueeze(1).broadcast_to([P, TOK, V_DIM]),
                                            0.0, None, ALU.mult).then_inc(v_zero, 1)
            pool.wait_ge(gated, KD)
            for m in range(KD):
                pool.wait_ge(mla_gated, m + 1)
                if m >= 2:
                    pool.wait_ge(merged_lo_done, m - 1)
                nc.gpsimd.tensor_tensor(h32[:, m % 2, :], tanh_mla[:, m, :], br_pool[:, m, :], ALU.add)\
                    .then_inc(merged_ready, 1)
            squares_up(2)
            norm(2)


def kernel(x, c, positions, w_ada, b_ada, norm_ffn1, w_ffn1_in, w_ffn1_out,
           norm_mix, w_in, pool_grp, pool_scale, w_pool_proj, q_a_norm, w_q_up,
           kv_a_norm, w_kv_up, q_norm_nope, q_norm_rope, k_norm_nope, k_norm_rope,
           w_mla_proj, w_out, norm_ffn2, w_ffn2_in, w_ffn2_out):
    import numpy as np
    import concourse.bacc as bacc
    from concourse.bass_utils import run_bass_kernel_spmd

    def cols(v):
        return np.asarray(v).reshape(-1, P).T

    ffn_in = [np.asarray(w)[0].reshape(KD, P, 2, NF, P).transpose(3, 1, 2, 0, 4).reshape(NF, P, IN_ELEMS)
              for w in (w_ffn1_in, w_ffn2_in)]
    ffn_out = [np.asarray(w)[0].reshape(2, NFH, P, KD, P).transpose(3, 0, 2, 1, 4).reshape(2 * KD, P, OUT_ELEMS)
               for w in (w_ffn1_out, w_ffn2_out)]
    w = np.asarray(w_in)[0]
    at = np.cumsum([0, 512, LAT, D, D])
    kv = np.asarray(w_kv_up)[0].reshape(KV_TILES, P, HEADS, 2, NOPE).transpose(1, 0, 3, 2, 4).reshape(P, -1)
    q_up = np.asarray(w_q_up)[0].reshape(Q_TILES, P, 2, 384).transpose(2, 1, 0, 3).reshape(2, P, -1)
    grp = np.asarray(pool_grp)[0].transpose(1, 0, 2).reshape(P, -1)

    def tiles(m, per_chunk):
        kt, mt = m.shape[0] // P, m.shape[1] // P
        return list(m.reshape(kt, P, mt // per_chunk, per_chunk, P).transpose(2, 1, 3, 0, 4)
                    .reshape(mt // per_chunk, P, per_chunk * kt * P))

    mix = [w[:, 512 + a:512 + a + n].reshape(KD, P, n).transpose(1, 0, 2).reshape(P, -1) for a, n in LAT_COLS]
    mix += tiles(w[:, 0:512], 2) + [kv, q_up[0], np.concatenate([q_up[1], grp], axis=1)]
    mix += tiles(np.asarray(w_pool_proj)[0], 4) + tiles(w[:, at[2]:at[4]], 2)
    mix += tiles(np.asarray(w_mla_proj)[0], 4) + tiles(np.asarray(w_out)[0], 2)
    w_mix = np.zeros((len(mix), P, SLOT), np.float32)
    for n, m in enumerate(mix):
        assert m.shape[1] == MIX_SIZES[n]
        w_mix[n, :, 0:m.shape[1]] = m
    tok = np.arange(P)
    mask = np.where(tok[None, :] <= tok[:, None], np.float32(0), np.float32(-1e30))
    first = np.arange(1, 17)
    corr = np.concatenate([(2 << g) / np.minimum(first, 2 << g) for g in range(POOL_TILES)])
    freq = np.float32(10000.0) ** (-np.arange(0, ROPE, 2, dtype=np.float32) / np.float32(ROPE))
    rows = [np.asarray(v)[0] for v in (q_norm_nope, q_norm_rope, k_norm_nope, k_norm_rope)]
    mix_consts = np.concatenate(
        [mask] + [np.broadcast_to(v.astype(np.float32), (P, len(v))) for v in (*rows, corr, freq)]
        + [cols(v[0]) for v in (q_a_norm, kv_a_norm, pool_scale)], axis=1)
    arrays = {
        "x_t": np.asarray(x)[0].T.reshape(KD, P, S).transpose(1, 0, 2),
        "c_t": cols(c[0]),
        "gains": np.concatenate([cols(g[0]) for g in (norm_ffn1, norm_mix, norm_ffn2)], axis=1),
        "b_ada": cols(b_ada[0]),
        "w_ada": np.asarray(w_ada)[0].reshape(KD, P, ADA_GROUPS, ADA_COLS).transpose(2, 0, 1, 3),
        "w_ffn_in": np.stack(ffn_in),
        "w_ffn_out": np.stack(ffn_out),
        "w_mix": w_mix,
        "mix_consts": mix_consts,
        "positions": np.asarray(positions)[0].reshape(TOK, P).T,
        "consts": np.eye(P, dtype=np.float32),
    }
    arrays = {n: np.ascontiguousarray(a) for n, a in arrays.items()}
    nc = bacc.Bacc("TRN2", target_bir_lowering=False, num_devices=1)
    args = [nc.dram_tensor(n, a.shape, mybir.dt.from_np(a.dtype), kind="ExternalInput").ap() for n, a in arrays.items()]
    out = nc.dram_tensor("out", (KD, P, S), F32, kind="ExternalOutput").ap()
    program(nc, *args, out)
    got = run_bass_kernel_spmd(nc, [arrays], core_ids=[0]).results[0]["out"]
    return np.ascontiguousarray(got.reshape(D, S).T)[None]
```
